# Optimizing a Trainium2 kernel written in Bass

```python
import jax, jax.numpy as jnp
from jax import lax
import numpy as np

D_MODEL = 1024
BATCH = 1
SEQ = 1024
DEPTH = 2

HEAD_DIM = 128
HEADS_PER_GROUP = 4
ATT_PATTERNS = ((128, 1), (512, 4), (2048, 16))
N_GROUPS = 3
N_ATT_HEADS = N_GROUPS * HEADS_PER_GROUP
ATT_QKV_WIDTH = N_ATT_HEADS * HEAD_DIM
ATT_OUT_WIDTH = HEADS_PER_GROUP * HEAD_DIM
ATT_BLOCK = 64
NEG_INF = -1e30
LRU_WIDTH = D_MODEL
LRU_BLOCKS = 4
LRU_BLOCK_WIDTH = LRU_WIDTH // LRU_BLOCKS
CONV_WIDTH = 4
CONV_LEFT = 2
RG_C = 8.0
NORM_EPS = 1e-6
IN_WIDTH = 3 * ATT_QKV_WIDTH + ATT_OUT_WIDTH + 2 * LRU_WIDTH + 2 * D_MODEL

kernel_name = "hybrid_dilated_attn_rglru_encoder"

def rms_norm(x, g):
    x32 = x.astype(jnp.float32)
    y = x32 * lax.rsqrt(jnp.mean(x32 * x32, axis=-1, keepdims=True) + NORM_EPS)
    return (y * g.astype(jnp.float32)).astype(x.dtype)

def alibi_slopes():
    return 2.0 ** (-8.0 * jnp.arange(1, N_ATT_HEADS + 1, dtype=jnp.float32) / N_ATT_HEADS)

def dilated_window_attention(q, k, v, window, dilation, slopes):
    b, s, h, dh = q.shape
    half = window // (2 * dilation)
    c = ATT_BLOCK
    n = s // dilation
    nblk = -(-n // c)
    pad = nblk * c - n

    def strided(t):
        return t.reshape(b, n, dilation, h, dh).transpose(0, 2, 1, 3, 4)

    qs = jnp.pad(strided(q), ((0, 0), (0, 0), (0, pad), (0, 0), (0, 0))).reshape(b, dilation, nblk, c, h, dh)

    def band(t):
        tp = jnp.pad(strided(t), ((0, 0), (0, 0), (c, pad + c), (0, 0), (0, 0))).reshape(b, dilation, nblk + 2, c, h, dh)
        return jnp.concatenate([tp[:, :, :-2], tp[:, :, 1:-1], tp[:, :, 2:]], axis=3)

    kw, vw = band(k), band(v)
    scores = jnp.einsum('brnqhd,brnkhd->brnhqk', qs, kw, preferred_element_type=jnp.float32) * (dh ** -0.5)
    qi = jnp.arange(c)
    kj = jnp.arange(3 * c) - c
    delta = kj[None, :] - qi[:, None]
    key_idx = jnp.arange(nblk)[:, None] * c + kj[None, :]
    valid = (jnp.abs(delta) <= half)[None] & ((key_idx >= 0) & (key_idx < n))[:, None, :]
    dist = (jnp.abs(delta) * dilation).astype(jnp.float32)
    bias = -slopes.astype(jnp.float32)[:, None, None] * dist[None]
    scores = jnp.where(valid[:, None], scores + bias, NEG_INF)
    m = jnp.max(scores, axis=-1, keepdims=True)
    p = jnp.exp(scores - m)
    den = jnp.sum(p, axis=-1, keepdims=True)
    out = jnp.einsum('brnhqk,brnkhd->brnqhd', p / den, vw.astype(jnp.float32))
    lse = (m + jnp.log(den))[..., 0].transpose(0, 1, 2, 4, 3)

    def unstride(t):
        t = t.reshape((b, dilation, nblk * c) + t.shape[4:])[:, :, :n]
        t = jnp.moveaxis(t, 1, 2)
        return t.reshape((b, s) + t.shape[3:])

    return unstride(out), unstride(lse)

def dilated_attention_mixer(q, k, v):
    b, s, _ = q.shape
    shp = (b, s, N_GROUPS, HEADS_PER_GROUP, HEAD_DIM)
    q, k, v = q.reshape(shp), k.reshape(shp), v.reshape(shp)
    slopes = alibi_slopes().reshape(N_GROUPS, HEADS_PER_GROUP)
    outs, lses = [], []
    for g, (window, dilation) in enumerate(ATT_PATTERNS):
        o, l = dilated_window_attention(q[:, :, g], k[:, :, g], v[:, :, g], window, dilation, slopes[g])
        outs.append(o)
        lses.append(l)
    outs = jnp.stack(outs, axis=0)
    alpha = jax.nn.softmax(jnp.stack(lses, axis=0), axis=0)
    mixed = jnp.sum(alpha[..., None] * outs, axis=0)
    return mixed.reshape(b, s, ATT_OUT_WIDTH).astype(q.dtype)

def centred_depthwise_conv(x, w, bias):
    s = x.shape[1]
    xp = jnp.pad(x, ((0, 0), (CONV_LEFT, CONV_WIDTH - 1 - CONV_LEFT), (0, 0)))
    y = bias + xp[:, 0:s] * w[0]
    for j in range(1, CONV_WIDTH):
        y = y + xp[:, j:j + s] * w[j]
    return y

def block_diag_linear(x, w, b):
    xr = x.reshape(x.shape[:-1] + (LRU_BLOCKS, LRU_BLOCK_WIDTH))
    return jnp.einsum('bsni,nij->bsnj', xr, w).reshape(x.shape) + b

def _linear_combine(left, right):
    a1, b1 = left
    a2, b2 = right
    return a1 * a2, a2 * b1 + b2

def rg_lru(x, w_a, b_a, w_x, b_x, lam, reverse):
    s = x.shape[1]
    r = jax.nn.sigmoid(block_diag_linear(x, w_a, b_a)).astype(jnp.float32)
    i = jax.nn.sigmoid(block_diag_linear(x, w_x, b_x))
    log_a = -RG_C * r * jax.nn.softplus(-lam.astype(jnp.float32))
    a = jnp.exp(log_a)
    mult = jnp.sqrt(-jnp.expm1(2.0 * log_a))
    first = (jnp.arange(s) == (s - 1 if reverse else 0))[None, :, None]
    mult = jnp.where(first, 1.0, mult)
    bterm = mult * (i * x).astype(jnp.float32)
    _, h = lax.associative_scan(_linear_combine, (a, bterm), axis=1, reverse=reverse)
    return h

def recurrent_mixer(x, conv_w, conv_b, w_a, b_a, w_x, b_x, lam):
    xc = centred_depthwise_conv(x, conv_w, conv_b)
    h = rg_lru(xc, w_a[0], b_a[0], w_x[0], b_x[0], lam[0], False) + \
        rg_lru(xc, w_a[1], b_a[1], w_x[1], b_x[1], lam[1], True)
    return h.astype(x.dtype)

def hybrid_layer(x, norm_g, w_in, b_gate, conv_w, conv_b, rg_w_a, rg_b_a, rg_w_x, rg_b_x, rg_lam,
                 w_o_att, w_o_lru, w_out):
    xn = rms_norm(x, norm_g)
    proj = xn @ w_in
    widths = [ATT_QKV_WIDTH, ATT_QKV_WIDTH, ATT_QKV_WIDTH, ATT_OUT_WIDTH, LRU_WIDTH, LRU_WIDTH]
    cuts = [int(c) for c in np.cumsum(widths)]
    q, k, v, g_att, x_lru, g_lru, gate_logits = jnp.split(proj, cuts, axis=-1)
    y_att = dilated_attention_mixer(q, k, v) * jax.nn.silu(g_att)
    y_lru = recurrent_mixer(x_lru, conv_w, conv_b, rg_w_a, rg_b_a, rg_w_x, rg_b_x, rg_lam) * jax.nn.silu(g_lru)
    gates = jax.nn.sigmoid(gate_logits + b_gate)
    gate_att, gate_lru = gates[..., :D_MODEL], gates[..., D_MODEL:]
    merged = gate_att * (y_att @ w_o_att) + gate_lru * (y_lru @ w_o_lru)
    return x + merged @ w_out

def setup_inputs(seed: int = 0) -> dict:
    key = jax.random.key(seed)
    ks = jax.random.split(key, 16)
    f32 = jnp.float32
    nrm = lambda k, shp, scale: jax.random.normal(k, shp, f32) * scale
    a_init = jax.random.uniform(ks[11], (DEPTH, 2, LRU_WIDTH), f32, 0.9, 0.999)
    p0 = a_init ** (1.0 / RG_C)
    return {
        "x": nrm(ks[0], (BATCH, SEQ, D_MODEL), 1.0),
        "norm_g": 1.0 + nrm(ks[1], (DEPTH, D_MODEL), 0.1),
        "w_in": nrm(ks[2], (DEPTH, D_MODEL, IN_WIDTH), D_MODEL ** -0.5),
        "b_gate": nrm(ks[3], (DEPTH, 2 * D_MODEL), 0.1),
        "conv_w": nrm(ks[4], (DEPTH, CONV_WIDTH, LRU_WIDTH), CONV_WIDTH ** -0.5),
        "conv_b": nrm(ks[5], (DEPTH, LRU_WIDTH), 0.05),
        "rg_w_a": nrm(ks[6], (DEPTH, 2, LRU_BLOCKS, LRU_BLOCK_WIDTH, LRU_BLOCK_WIDTH), LRU_BLOCK_WIDTH ** -0.5),
        "rg_b_a": nrm(ks[7], (DEPTH, 2, LRU_WIDTH), 0.1),
        "rg_w_x": nrm(ks[8], (DEPTH, 2, LRU_BLOCKS, LRU_BLOCK_WIDTH, LRU_BLOCK_WIDTH), LRU_BLOCK_WIDTH ** -0.5),
        "rg_b_x": nrm(ks[9], (DEPTH, 2, LRU_WIDTH), 0.1),
        "rg_lam": jnp.log(p0) - jnp.log1p(-p0),
        "w_o_att": nrm(ks[12], (DEPTH, ATT_OUT_WIDTH, D_MODEL), ATT_OUT_WIDTH ** -0.5),
        "w_o_lru": nrm(ks[13], (DEPTH, LRU_WIDTH, D_MODEL), LRU_WIDTH ** -0.5),
        "w_out": nrm(ks[14], (DEPTH, D_MODEL, D_MODEL), D_MODEL ** -0.5),
        "final_g": 1.0 + nrm(ks[15], (D_MODEL,), 0.1),
    }

def reference(x, norm_g, w_in, b_gate, conv_w, conv_b, rg_w_a, rg_b_a, rg_w_x, rg_b_x, rg_lam,
              w_o_att, w_o_lru, w_out, final_g):
    for l in range(DEPTH):
        x = hybrid_layer(x, norm_g[l], w_in[l], b_gate[l], conv_w[l], conv_b[l], rg_w_a[l], rg_b_a[l],
                         rg_w_x[l], rg_b_x[l], rg_lam[l], w_o_att[l], w_o_lru[l], w_out[l])
    return rms_norm(x, final_g)


_drawn_inputs = setup_inputs


def setup_inputs(seed=0):
    import zlib

    import numpy as np

    out = dict(_drawn_inputs(seed))
    spreads = {}
    factors = {'rg_b_a': 5.793, 'rg_b_x': 3.164}
    for name, (base, spread) in spreads.items():
        noise = np.random.default_rng([zlib.crc32(name.encode()), seed]).standard_normal(out[name].shape)
        drawn = base * np.exp(spread * noise) if base else spread * noise
        out[name] = __import__('jax').numpy.asarray(drawn.astype(out[name].dtype))
    for name, factor in factors.items():
        out[name] = (out[name] * factor).astype(out[name].dtype)
    return out
```

```python
from contextlib import ExitStack

import numpy as np

import concourse.bass as bass
from concourse import mybir

ALU = mybir.AluOpType
ACT = mybir.ActivationFunctionType
F32 = mybir.dt.float32
F32R = mybir.dt.float32r

P = 128
D_MODEL, SEQ, DEPTH = 1024, 1024, 2
KT = D_MODEL // P
HALF = 512
HEADS_PER_GROUP, N_GROUPS, HEAD_DIM = 4, 3, 128
QKV = N_GROUPS * HEADS_PER_GROUP * HEAD_DIM
ATT_OUT = HEADS_PER_GROUP * HEAD_DIM
ATT_KT = ATT_OUT // P
DILATION = (1, 4, 16)
WINDOW_HALF = 64
BLOCKS, BLOCK_W, CONV_W = 4, 256, 4
TPB = BLOCK_W // P
EPS = 1e-6
SCALE = float(HEAD_DIM) ** -0.5
MASKED = -1e30

PAR_NORM, PAR_CONV, PAR_CONV_B, PAR_GATE, PAR_RGA, PAR_RGX, PAR_LAM, N_PAR = 0, 8, 40, 48, 64, 80, 96, 112
HALF_GATT, HALF_GLRU, HALF_RGA, HALF_RGX, N_HALF = 0, 8, 16, 32, 48

PHASES = (("PRE", 1), ("LRU", 3), ("LRUL", 1), ("LMIX", 3), ("LMIXL", 1), ("QK", 1), ("ATT", 3), ("ATTL", 1),
          ("AMIX", 3), ("AMIXL", 1), ("WOUT", 3), ("WOUTL", 1))


def phases(**n):
    return {name: n.get(name, 0) for name, _ in PHASES}


JOBS = phases(PRE=2, LRU=6, LRUL=6, LMIX=4, LMIXL=2, QK=2, ATT=10, ATTL=10, AMIX=4, AMIXL=2, WOUT=2, WOUTL=2)
N_JOBS = sum(JOBS[name] * times for name, times in PHASES)


class Count:

    def __init__(self, sem, per, head=0, by=1):
        self.sem, self.per, self.head, self.by = sem, per, head, by
        self.start, total = {}, 0
        for name, times in PHASES:
            self.start[name] = total
            total += per[name] * times
        self.layer = total

    def after(self, l, phase, i, k):
        return (l * self.layer + i * self.per[phase] + (self.start[phase] + k)) * self.by + self.head


def units():
    mid0 = [(0, "mid", i, 256, i) for i in range(7)]
    mid1 = [(1, "mid", r, 256, 8 + r) for r in range(4)]
    edge1 = [(1, "edge", r, 128, 12 + r) for r in range(4)]
    full2 = [(2, "full", j, 128, 16 + j) for j in range(8)]
    banks = [[mid0[0], (0, "edge", 0, 128, 7)], mid0[1:3], mid0[3:5], mid0[5:7], mid1[0:2], mid1[2:4], edge1,
             full2[0:4], full2[4:8]]
    out = []
    for tiles in banks:
        column, bank = 0, []
        for g, kind, i, width, stat in tiles:
            bank.append((g, kind, i, column, width, stat))
            column += width
        out.append(bank)
    return out


UNITS = units()
UNITS_OF = [range(0, 4), range(4, 7), range(7, 9)]
N_UNITS = len(UNITS)
N_STATS = 24
SCORES_AT, VT_AT, PT_AT = [0, 6, 11], [4, 9, 13], 15
BANK_USES = PT_AT + N_UNITS
BIAS_AT = {(0, "mid"): 0, (0, "edge"): 256, (1, "mid"): 384, (1, "edge"): 640, (2, "full"): 768}
N_BIAS = 896


def job_columns():
    x_at, glru_at = 3 * QKV + ATT_OUT, 3 * QKV + ATT_OUT + D_MODEL
    gate_at = glru_at + D_MODEL
    x = lambda b: [("w_in", x_at + (TPB * b + t) * P) for t in range(TPB)]
    gate = lambda which, m: ("w_in", gate_at + which * D_MODEL + m * P)
    qkv = lambda which, g, h: ("w_in", which * QKV + (g * HEADS_PER_GROUP + h) * HEAD_DIM)
    jobs = x(0)
    for b in range(BLOCKS):
        jobs += [("w_in", glru_at + (TPB * b + t) * P) for t in range(TPB)] + [("rg", b, 0), ("rg", b, 1)]
        jobs += x(b + 1) if b + 1 < BLOCKS else [gate(1, 0), gate(1, 1)]
    for i in range(KT // 2):
        jobs += [("w_o_lru", (2 * i + t) * P) for t in range(2)]
        jobs += [gate(1, 2 * i + 2), gate(1, 2 * i + 3)] if 2 * i + 2 < KT else []
    jobs += [qkv(0, 0, 0), qkv(1, 0, 0)]
    for h in range(HEADS_PER_GROUP):
        jobs += [qkv(2, 0, h)] + [qkv(w, g, h) for g in (1, 2) for w in range(3)] + [("w_in", 3 * QKV + h * HEAD_DIM)]
        jobs += [qkv(0, 0, h + 1), qkv(1, 0, h + 1)] if h + 1 < HEADS_PER_GROUP else [gate(0, 0), gate(0, 1)]
    for i in range(KT // 2):
        jobs += [("w_o_att", (2 * i + t) * P) for t in range(2)]
        jobs += [gate(0, 2 * i + 2), gate(0, 2 * i + 3)] if 2 * i + 2 < KT else []
    return jobs + [("w_out", m * P) for m in range(KT)]


def build(nc, xT, blocks, params, final_g, bias_table, identity, outT):
    with ExitStack() as ctx:
        names = [0]

        def sem(name):
            names[0] += 1
            return ctx.enter_context(nc.semaphore(name))

        def count(name, head=0, by=1, **per):
            return Count(sem(name), phases(**per), head, by)

        def counts(name, head=0, by=1, **per):
            return Count(sem(name), per, head, by)

        half_jobs = {name: n // 2 for name, n in JOBS.items()}
        dense = dict(JOBS, LRU=4, LRUL=4)
        raw_in = [counts(f"raw_in{p}", by=16, **half_jobs) for p in range(2)]
        w_hi = counts("w_hi", **JOBS)
        w_lo = counts("w_lo", head=2, **JOBS)
        job_done = counts("job_done", **dense)
        rg_done = count("rg_done", LRU=8, LRUL=8)
        norm_done = count("norm_done", PRE=2)
        pair_free = [
            count("pair_free0", head=1, PRE=2, LRU=4, LRUL=4, LMIX=2, LMIXL=1, QK=1, ATT=5, ATTL=5, AMIX=2, AMIXL=1,
                  WOUT=1, WOUTL=1),
            count("pair_free1", head=1, PRE=1, LRU=4, LRUL=4, LMIX=2, LMIXL=1, QK=1, ATT=6, ATTL=6, AMIX=2, AMIXL=1,
                  WOUT=1, WOUTL=1),
            count("pair_free2", head=1, LRU=2, LRUL=2),
            count("pair_free3", head=1, LRU=2, LRUL=2, ATT=2, ATTL=2),
        ]
        bank_free = [count(f"bank_free{n}", head=1, ATT=BANK_USES // 2, ATTL=BANK_USES // 2) for n in range(2)]
        x_in = [sem(f"x_in{n}") for n in range(KT)]
        sq_ready = count("sq_ready", head=KT, WOUT=2, WOUTL=2)
        sumsq_step = count("sumsq_step", head=KT + 1, WOUT=2, WOUTL=2, AMIXL=1)
        norm_step = count("norm_step", PRE=2)
        xf_ready = count("xf_ready", PRE=KT)
        xh_ready = count("xh_ready", PRE=KT)
        xl_dve = count("xl_dve", PRE=KT // 2)
        xl_pool = count("xl_pool", PRE=KT // 2)
        fin_ready = sem("fin_ready")
        x_kept = count("x_kept", by=16, PRE=KT)
        par_step = count("par_step", PRE=20)
        lam_exp = count("lam_exp", PRE=1)
        conv_init = count("conv_init", PRE=2, LRU=2)
        conv_step = count("conv_step", PRE=4, LRU=4)
        xc_hi = count("xc_hi", PRE=2, LRU=2)
        xc_lo = count("xc_lo", PRE=2, LRU=2)
        silu_tanh = count("silu_tanh", LRU=2, LRUL=2, ATT=1, ATTL=1)
        decay_ready = count("decay_ready", LRU=4, LRUL=4)
        half_decay = count("half_decay", LRU=4, LRUL=4)
        root_ready = count("root_ready", LRU=4, LRUL=4)
        rec_step = count("rec_step", LRU=20, LRUL=20)
        y_hi = count("y_hi", LRU=2, LRUL=2)
        y_lo = count("y_lo", head=1, LRU=2, LRUL=2)
        unit_ready = count("unit_ready", ATT=BANK_USES, ATTL=BANK_USES)
        qkv_ready = count("qkv_ready", QK=2, ATT=9, ATTL=7)
        bias_in = count("bias_in", head=16, by=16, ATT=1, ATTL=1)
        max_out = count("max_out", by=16, ATT=8, ATTL=8)
        max_in = count("max_in", by=16, ATT=1, ATTL=1)
        max_step = count("max_step", ATT=3, ATTL=3)
        negmax_out = count("negmax_out", by=16, ATT=1, ATTL=1)
        negmax_in = count("negmax_in", by=16, ATT=8, ATTL=8)
        exp_done = count("exp_done", ATT=N_UNITS, ATTL=N_UNITS)
        den_out = count("den_out", by=16, ATT=8, ATTL=8)
        den_in = count("den_in", by=16, ATT=1, ATTL=1)
        den_step = count("den_step", ATT=3, ATTL=3)
        rden_out = count("rden_out", by=16, ATT=1, ATTL=1)
        rden_in = count("rden_in", by=16, ATT=1, ATTL=1)
        pv_done = count("pv_done", ATT=3, ATTL=3)
        asm_step = count("asm_step", head=1, ATT=3, ATTL=3)
        asm_start = count("asm_start", ATT=1, ATTL=1)
        ya_hi = count("ya_hi", ATT=1, ATTL=1)
        ya_lo = count("ya_lo", ATT=1, ATTL=1)
        mix_done = count("mix_done", AMIX=2, AMIXL=2)
        mh_ready = count("mh_ready", AMIXL=KT)
        ml_ready = count("ml_ready", AMIXL=KT)
        xold_in = [count(f"xold_in{p}", by=16, WOUT=1, WOUTL=1) for p in range(2)]
        const_in = sem("const_in")
        started = sem("started")
        out_done = sem("out_done")

        KB = 1024
        base = (nc.sbuf_base + 63) // 64 * 64
        at = [base]

        def place(name, shape, dtype=F32, offset=None):
            size = int(np.prod(shape[1:])) * 4
            if offset is None:
                offset = at[0]
                at[0] += (size + 31) // 32 * 32
            assert offset + size <= nc.sbuf_usable_end, (name, offset + size)
            return nc.alloc_sbuf_tensor_at(name, shape, dtype, offset=offset)

        def region(kilobytes):
            at[0] += kilobytes * KB
            return at[0] - kilobytes * KB

        raw = place("raw", [P, 2, KT * P])
        wh = place("wh", [P, 2, KT * P], F32R)
        wl = place("wl", [P, 2, KT * P], F32R)
        xh = place("xh", [P, KT, SEQ], F32R)
        xl = place("xl", [P, KT, SEQ], F32R)
        m_at = region(32)
        stream = place("stream", [P, KT, SEQ], offset=m_at)
        decay = place("decay", [P, 2, SEQ], offset=m_at)
        root0 = place("root0", [P, 2, SEQ], offset=m_at + 8 * KB)
        gated0 = place("gated0", [P, 2, SEQ], offset=m_at + 16 * KB)
        hsum = place("hsum", [P, 2, SEQ], offset=m_at + 24 * KB)
        y_at = region(64)
        yh = place("yh", [P, KT, SEQ], F32R, offset=y_at)
        yl = place("yl", [P, KT, SEQ], F32R, offset=y_at + 32 * KB)
        yah = place("yah", [P, ATT_KT, SEQ], F32R, offset=y_at)
        yal = place("yal", [P, ATT_KT, SEQ], F32R, offset=y_at + 16 * KB)
        scores = place("scores", [P, N_UNITS, HALF], offset=y_at + 32 * KB)
        values = place("values", [P, N_GROUPS, KT, P], offset=y_at + 32 * KB + N_UNITS * 2 * KB)
        t_at = region(32)
        xc = place("xc", [P, 2, SEQ], offset=t_at)
        silu = place("silu", [P, 2, SEQ], offset=t_at + 8 * KB)
        root1 = place("root1", [P, 2, SEQ], offset=t_at + 16 * KB)
        gated1 = place("gated1", [P, 2, SEQ], offset=t_at + 24 * KB)
        gate = place("gate", [P, 2, SEQ], offset=t_at)
        qT = place("qT", [P, SEQ], offset=t_at)
        kT = place("kT", [P, SEQ], offset=t_at + 4 * KB)
        vT = place("vT", [P, SEQ], offset=t_at + 8 * KB)
        pT = place("pT", [P, 3, HALF], offset=t_at + 12 * KB)
        acc = place("acc", [P, SEQ], offset=t_at + 20 * KB)
        rden = place("rden", [P, SEQ], offset=t_at + 24 * KB)
        silu_a = place("silu_a", [P, SEQ], offset=t_at + 28 * KB)
        xf = place("xf", [P, 2, SEQ], offset=t_at)
        xold = place("xold", [P, 2, SEQ], offset=t_at + 8 * KB)
        sq = place("sq", [P, 2, SEQ], offset=t_at + 16 * KB)
        sumsq = place("sumsq", [P, SEQ], offset=t_at + 24 * KB)
        diag = place("diag", [P, KT, P], offset=t_at + 28 * KB)
        lam_t = place("lam_t", [P, 6, 2 * KT], offset=t_at + 8 * KB)
        bias = place("bias", [P, N_BIAS])
        ident = place("ident", [P, P])
        ones = place("ones", [P, P])
        par_all = place("par_all", [P, DEPTH, N_PAR])
        par = place("par", [P, N_PAR])
        half = place("half", [P, N_HALF])
        decay_k = place("decay_k", [P, 2 * KT])
        half_k = place("half_k", [P, 2 * KT])
        gfin = place("gfin", [P, KT])
        eps = place("eps", [P, 1])
        rms = place("rms", [P, KT])
        rinv = place("rinv", [P, KT])
        rowmax = place("rowmax", [P, N_STATS])
        negmax = place("negmax", [P, N_STATS])
        den = place("den", [P, N_STATS])
        stat_c = place("stat_c", [P, N_GROUPS, KT])
        stat_t = place("stat_t", [P, 3, KT])

        pair = [ctx.enter_context(nc.psum_tensor(f"pair{n}", [P, SEQ], F32)) for n in range(4)]
        bank = [pair[2][:, n * HALF:(n + 1) * HALF] for n in range(2)]

        kept = nc.dram_tensor("kept", [KT, P, SEQ], F32, kind="Internal").ap()
        max_d = nc.dram_tensor("max_d", [N_GROUPS, SEQ], F32, kind="Internal").ap()
        den_d = nc.dram_tensor("den_d", [N_GROUPS, SEQ], F32, kind="Internal").ap()
        negmax_d = nc.dram_tensor("negmax_d", [1, SEQ], F32, kind="Internal").ap()
        rden_d = nc.dram_tensor("rden_d", [1, SEQ], F32, kind="Internal").ap()

        def hold(engine, semaphore, value):
            if not isinstance(value, int):
                value = engine.to_reg(value)
            engine.wait_ge(started, 1)
            engine.wait_ge(semaphore, value)

        def one(i):
            return slice(i, i + 1) if isinstance(i, int) else bass.ds(i, 1)

        def col(table, i):
            return table[:, one(i)]

        def tile_of(tensor, i):
            return tensor[:, i, :] if isinstance(i, int) else tensor[:, bass.ds(i, 1), :].rearrange("p a s -> p (a s)")

        def stat_pieces(table, rows):
            g0, g1, g2 = rows
            by_token = g2.rearrange("(n b j) -> b n j", b=2, j=KT)
            return [
                (table[:, 0:7], g0[64:960].rearrange("(c p) -> p c", p=P)),
                (table[0:64, 7:8], g0[960:1024].rearrange("(p c) -> p c", c=1)),
                (table[64:128, 7:8], g0[0:64].rearrange("(p c) -> p c", c=1)),
                (table[:, 8:12], g1[256:768].rearrange("(p r) -> p r", r=4)),
                (table[0:64, 12:16], g1[768:1024].rearrange("(p r) -> p r", r=4)),
                (table[64:128, 12:16], g1[0:256].rearrange("(p r) -> p r", r=4)),
                (table[0:64, 16:24], by_token[0]),
                (table[64:128, 16:24], by_token[1]),
            ]

        def by_group(g, ap):
            if g == 0:
                return ap
            if g == 1:
                return ap.rearrange("p (n r) -> p r n", r=4)
            return ap.rearrange("p (n b j) -> p j b n", b=2, j=8)

        def in_group(g, ap):
            if g == 0:
                return ap
            if g == 1:
                return ap.rearrange("p (r n) -> p r n", r=4)
            return ap.rearrange("p (j b n) -> p j b n", b=2, j=8)

        block = ctx.enter_context(nc.Block())

        @block.sync
        def _(sp):
            for n in range(KT):
                sp.dma_start(stream[:, n, :], xT[n]).then_inc(x_in[n], 16)
            sp.dma_start(ident[:], identity).then_inc(const_in, 16)
            sp.dma_start(par_all[:], params).then_inc(const_in, 16)
            sp.dma_start(gfin[:], final_g).then_inc(const_in, 16)
            sp.dma_start(bias[:], bias_table[0]).then_inc(bias_in.sem, 16)

            def load(l, phase, i, k, width=KT * P):
                start = JOBS_START[phase]
                j = l * N_JOBS + i * JOBS[phase] + (start + k)
                hold(sp, w_lo.sem, w_lo.after(l, phase, i, k - 1))
                src = blocks[j] if isinstance(j, int) else blocks[bass.ds(j, 1)].rearrange("a p c -> (a p) c")
                sp.dma_start(raw[:, k % 2, 0:width], src[:, 0:width]).then_inc(raw_in[k % 2].sem, 16)

            def keep_stream(l):
                hold(sp, sumsq_step.sem, sumsq_step.after(l, "PRE", 0, 0))
                for n in range(KT):
                    sp.dma_start(kept[n], stream[:, n, :]).then_inc(x_kept.sem, 16)

            def load_old(l, phase, i):
                for p in range(2):
                    if phase == "WOUT":
                        hold(sp, pair_free[p].sem, pair_free[p].after(l, phase, i, 0))
                        n = i * 2 + p
                    else:
                        hold(sp, pair_free[p].sem, pair_free[p].after(l, phase, 0, 0))
                        n = KT - 2 + p
                    src = kept[n] if isinstance(n, int) else kept[bass.ds(n, 1)].rearrange("a p s -> (a p) s")
                    sp.dma_start(xold[:, p, :], src).then_inc(xold_in[p].sem, 16)

            def exchange_max(l, phase, h, next_bias):
                for use in (SCORES_AT[2], SCORES_AT[2] + 1):
                    b = bank_free[use % 2]
                    hold(sp, b.sem, b.after(l, phase, h, use // 2 + 1))
                for sbuf, dram in stat_pieces(rowmax, [max_d[g] for g in range(3)]):
                    sp.dma_start(dram, sbuf, allow_slow_non_contiguous=True).then_inc(max_out.sem, 16)
                sp.dma_start(bias[:], next_bias).then_inc(bias_in.sem, 16)
                hold(sp, max_out.sem, max_out.after(l, phase, h, 8))
                sp.dma_start(stat_c[:], max_d.rearrange("g (p i) -> p g i", i=KT)).then_inc(max_in.sem, 16)
                hold(sp, max_step.sem, max_step.after(l, phase, h, 3))
                sp.dma_start(negmax_d[0].rearrange("(p i) -> p i", i=KT), stat_t[:, 2, :]).then_inc(negmax_out.sem, 16)
                hold(sp, negmax_out.sem, negmax_out.after(l, phase, h, 1))
                for sbuf, dram in stat_pieces(negmax, [negmax_d[0]] * 3):
                    sp.dma_start(sbuf, dram, allow_slow_non_contiguous=True).then_inc(negmax_in.sem, 16)

            def exchange_den(l, phase, h):
                hold(sp, exp_done.sem, exp_done.after(l, phase, h, N_UNITS))
                for sbuf, dram in stat_pieces(den, [den_d[g] for g in range(3)]):
                    sp.dma_start(dram, sbuf, allow_slow_non_contiguous=True).then_inc(den_out.sem, 16)
                hold(sp, den_out.sem, den_out.after(l, phase, h, 8))
                sp.dma_start(stat_c[:], den_d.rearrange("g (p i) -> p g i", i=KT)).then_inc(den_in.sem, 16)
                hold(sp, den_step.sem, den_step.after(l, phase, h, 3))
                sp.dma_start(rden_d[0].rearrange("(p i) -> p i", i=KT), stat_t[:, 2, :]).then_inc(rden_out.sem, 16)
                hold(sp, rden_out.sem, rden_out.after(l, phase, h, 1))
                hold(sp, asm_step.sem, asm_step.after(l, phase, h, 0))
                sp.dma_start(rden[:], rden_d.broadcast_to([P, SEQ])).then_inc(rden_in.sem, 16)

            def loads(l, phase, i, ks, width=KT * P):
                for k in ks:
                    load(l, phase, i, k, width)

            with sp.Fori(0, DEPTH) as l:
                loads(l, "PRE", 0, range(2))
                keep_stream(l)
                with sp.Fori(0, 3) as b:
                    loads(l, "LRU", b, range(6))
                loads(l, "LRUL", 0, range(6))
                with sp.Fori(0, 3) as i:
                    loads(l, "LMIX", i, range(4))
                loads(l, "LMIXL", 0, range(2))
                loads(l, "QK", 0, range(2))
                loads(l, "ATT", 0, range(10))
                with sp.Fori(0, 2) as h:
                    loads(l, "ATT", h + 1, range(1))
                    exchange_max(l, "ATT", h, bias_table[bass.ds(h + 1, 1)].rearrange("a p c -> (a p) c"))
                    loads(l, "ATT", h + 1, range(1, 2))
                    exchange_den(l, "ATT", h)
                    loads(l, "ATT", h + 1, range(2, 10))
                loads(l, "ATTL", 0, range(1))
                exchange_max(l, "ATT", 2, bias_table[3])
                loads(l, "ATTL", 0, range(1, 2))
                exchange_den(l, "ATT", 2)
                loads(l, "ATTL", 0, range(2, 10))
                loads(l, "AMIX", 0, range(1), ATT_OUT)
                exchange_max(l, "ATTL", 0, bias_table[0])
                loads(l, "AMIX", 0, range(1, 2), ATT_OUT)
                exchange_den(l, "ATTL", 0)
                loads(l, "AMIX", 0, range(2, 4))
                with sp.Fori(1, 3) as i:
                    loads(l, "AMIX", i, range(2), ATT_OUT)
                    loads(l, "AMIX", i, range(2, 4))
                loads(l, "AMIXL", 0, range(2), ATT_OUT)
                with sp.Fori(0, 3) as i:
                    loads(l, "WOUT", i, range(2))
                    load_old(l, "WOUT", i)
                loads(l, "WOUTL", 0, range(2))
                load_old(l, "WOUTL", 0)
            for n in range(KT):
                sp.wait_ge(fin_ready, n + 1)
                sp.dma_start(outT[n], stream[:, n, :]).then_inc(out_done, 16)
            sp.wait_ge(out_done, 16 * KT)

        @block.scalar
        def _(act):
            def split_hi(l, phase, i, k, width=KT * P):
                r = raw_in[k % 2]
                act.wait_ge(r.sem, r.after(l, phase, i, k // 2 + 1))
                act.activation(wh[:, k % 2, 0:width], raw[:, k % 2, 0:width], ACT.Copy).then_inc(w_hi.sem, 1)

            def job(l, phase, i, k):
                act.wait_ge(job_done.sem, job_done.after(l, phase, i, k))

            def normalise(l, final=False):
                act.wait_ge(norm_done.sem, norm_done.after(l, "PRE", 0, 1))
                act.activation(rms[:], pair[0][:, 0:KT], ACT.Sqrt, bias=eps[:], scale=1.0 / D_MODEL)\
                    .then_inc(pair_free[0].sem, 1)
                if final:
                    return
                for k in range(KT):
                    act.wait_ge(xf_ready.sem, xf_ready.after(l, "PRE", 0, k + 1))
                    act.activation(xh[:, k, :], xf[:, k % 2, :], ACT.Copy).then_inc(xh_ready.sem, 1)

            def start_conv(l, phase, i, b, t):
                c = b * TPB + t
                act.activation(xc[:, t, :], pair[t][:], ACT.Identity, scale=col(par, c + (PAR_CONV + 2 * KT)),
                               bias=col(par, c + PAR_CONV_B)).then_inc(conv_init.sem, 1)

            def split_xc(l, phase, i, b, t, frees):
                act.wait_ge(pair_free[t].sem, pair_free[t].after(l, phase, i, frees))
                act.activation(tile_of(yh, b * TPB + t), xc[:, t, :], ACT.Copy).then_inc(xc_hi.sem, 1)

            def square(tile, p, step, n):
                act.activation(sq[:, p, :], tile, ACT.Square).then_inc(sq_ready.sem, 1)

            def rec_tanh(l, phase, i, b, o):
                d, t, which = o // 4, o // 2 % 2, o % 2
                q = (2 + o) % 4
                to = ((root0, gated0), (root1, gated1))[d][which]
                act.wait_ge(rg_done.sem, rg_done.after(l, phase, i, o + 1))
                bias_at = b * TPB + ((HALF_RGA, HALF_RGX)[which] + d * KT + t)
                act.activation(to[:, t, :], pair[q][:], ACT.Tanh, scale=0.5, bias=col(half, bias_at))\
                    .then_inc(pair_free[q].sem, 1)

            def rec_decay(l, phase, i, b, d):
                root = (root0, root1)[d]
                for t in range(2):
                    q = (2 + d * 4 + t * 2) % 4
                    act.wait_ge(pair_free[q].sem, pair_free[q].after(l, phase, i, RG_FREES[d * 4 + t * 2]))
                    if d == 1:
                        act.wait_ge(rec_step.sem, rec_step.after(l, phase, i, 9 + t))
                    k = b * TPB + (d * KT + t)
                    act.activation(decay[:, t, :], root[:, t, :], ACT.Exp, scale=col(decay_k, k), bias=col(decay_k, k))\
                        .then_inc(decay_ready.sem, 1)
                for t in range(2):
                    k = b * TPB + (d * KT + t)
                    act.activation(root[:, t, :], root[:, t, :], ACT.Tanh, scale=col(half_k, k), bias=col(half_k, k))\
                        .then_inc(half_decay.sem, 1)

            def rec_root(l, phase, i, d):
                root = (root0, root1)[d]
                act.wait_ge(half_decay.sem, half_decay.after(l, phase, i, 2 * d + 2))
                for t in range(2):
                    act.activation(root[:, t, :], root[:, t, :], ACT.Sqrt).then_inc(root_ready.sem, 1)

            def silu_start(l, phase, i, t):
                job(l, phase, i, t + 1)
                act.activation(silu[:, t, :], pair[t][:], ACT.Tanh, scale=0.5).then_inc(silu_tanh.sem, 1)

            def merge_gate(l, branch, m, p):
                act.activation(gate[:, p, :], pair[p][:], ACT.Tanh, scale=0.5,
                               bias=col(half, m + (HALF_GATT, HALF_GLRU)[branch])).then_inc(pair_free[p].sem, 1)

            def lru(l, phase, i, b, last):
                for t in range(2):
                    silu_start(l, phase, i, t)
                    split_hi(l, phase, i, t + 2)
                for o in range(4):
                    rec_tanh(l, phase, i, b, o)
                split_hi(l, phase, i, 4)
                rec_decay(l, phase, i, b, 0)
                for o in range(4, 8):
                    rec_tanh(l, phase, i, b, o)
                split_hi(l, phase, i, 5)
                rec_root(l, phase, i, 0)
                act.wait_ge(rec_step.sem, rec_step.after(l, phase, i, 4))
                job(l, phase, i, 3)
                if last:
                    merge_gate(l, 1, 0, 0)
                    split_hi(l, "LMIX", 0, 0)
                else:
                    start_conv(l, phase, i, b + 1, 0)
                    split_next(l, phase, i, 0)
                rec_decay(l, phase, i, b, 1)
                if not last:
                    split_xc(l, phase, i, b + 1, 0, PAIR_LRU[0])
                rec_root(l, phase, i, 1)
                job(l, phase, i, 4)
                if last:
                    merge_gate(l, 1, 1, 1)
                    split_hi(l, "LMIX", 0, 1)
                else:
                    start_conv(l, phase, i, b + 1, 1)
                    split_next(l, phase, i, 1)
                    split_xc(l, phase, i, b + 1, 1, PAIR_LRU[1])
                for t in range(2):
                    act.wait_ge(rec_step.sem, rec_step.after(l, phase, i, 18 + 2 * t))
                    act.activation(tile_of(yh, b * TPB + t), hsum[:, t, :], ACT.Copy).then_inc(y_hi.sem, 1)

            def split_next(l, phase, i, k):
                r = raw_in[k % 2]
                act.wait_ge(r.sem, r.after(l, phase, i + 1, k // 2 + 1))
                act.activation(wh[:, k % 2, :], raw[:, k % 2, :], ACT.Copy).then_inc(w_hi.sem, 1)

            def mix(l, phase, i, branch):
                width = KT * P
                for p in range(2):
                    job(l, phase, i, p + 1)
                    split_hi(l, phase, i, p + 2)
                for p in range(2):
                    job(l, phase, i, p + 3)
                    if branch:
                        act.wait_ge(pair_free[p].sem, pair_free[p].after(l, phase, i, 1))
                    else:
                        act.wait_ge(mix_done.sem, mix_done.after(l, phase, i, p + 1))
                    merge_gate(l, branch, i * 2 + (2 + p), p)
                    r = raw_in[p]
                    act.wait_ge(r.sem, r.after(l, phase, i + 1, 1))
                    act.activation(wh[:, p, 0:(ATT_OUT, width)[branch]], raw[:, p, 0:(ATT_OUT, width)[branch]],
                                   ACT.Copy).then_inc(w_hi.sem, 1)

            def qkv(l, phase, i, k, which, g, to, p):
                job(l, phase, i, k + 1)
                act.activation(in_group(g, to[:]), by_group(g, pair[p][:]), ACT.Copy,
                               scale=SCALE if which == "q" else 1.0).then_inc(pair_free[p].sem, 1)

            def take_values(l, phase, h, g):
                for n in range(2):
                    use = VT_AT[g] + n
                    act.wait_ge(unit_ready.sem, unit_ready.after(l, phase, h, use + 1))
                    act.activation(values[:, g, 4 * n:4 * n + 4, :].rearrange("p c d -> p (c d)"), bank[use % 2],
                                   ACT.Copy).then_inc(bank_free[use % 2].sem, 1)

            def exps(l, phase, h):
                act.wait_ge(negmax_in.sem, negmax_in.after(l, phase, h, 8))
                for u, tiles in enumerate(UNITS):
                    for n, (g, kind, idx, column, width, stat) in enumerate(tiles):
                        s = scores[:, u, column:column + width]
                        e = act.activation(s, s, ACT.Exp, bias=negmax[:, stat:stat + 1],
                                           accum_out=den[:, stat:stat + 1])
                    e.then_inc(exp_done.sem, 1)

            def assemble(l, phase, h):
                act.wait_ge(pv_done.sem, pv_done.after(l, phase, h, 1))
                act.activation(acc[:, 64:SEQ], pair[3][:, 0:SEQ - 64], ACT.Copy).then_inc(asm_start.sem, 1)
                act.activation(acc[:, 0:64], pair[3][:, SEQ - 64:SEQ], ACT.Copy).then_inc(pair_free[3].sem, 1)
                act.wait_ge(asm_step.sem, asm_step.after(l, phase, h, 3))
                slot = HEADS_PER_GROUP - 1 if phase == "ATTL" else h
                act.activation(tile_of(yah, slot), acc[:], ACT.Copy, scale=0.5).then_inc(ya_hi.sem, 1)

            def attention(l, phase, h, last):
                dst = {"q": qT, "k": kT, "v": vT}
                order = [("v", 0), ("q", 1), ("k", 1), ("v", 1), ("q", 2), ("k", 2), ("v", 2)]
                for k, (which, g) in enumerate(order):
                    qkv(l, phase, h, k, which, g, dst[which], k % 2)
                    split_hi(l, phase, h, k + 2)
                    if (which, g) == ("q", 1):
                        take_values(l, phase, h, 0)
                    if (which, g) == ("q", 2):
                        take_values(l, phase, h, 1)
                job(l, phase, h, 8)
                act.activation(silu_a[:], pair[1][:], ACT.Tanh, scale=0.5).then_inc(silu_tanh.sem, 1)
                split_hi(l, phase, h, 9)
                take_values(l, phase, h, 2)
                exps(l, phase, h)
                if last:
                    job(l, phase, h, 9)
                    merge_gate(l, 0, 0, 0)
                    split_hi(l, "AMIX", 0, 0, ATT_OUT)
                    assemble(l, phase, h)
                    job(l, phase, h, 10)
                    merge_gate(l, 0, 1, 1)
                    split_hi(l, "AMIX", 0, 1, ATT_OUT)
                else:
                    qkv(l, phase, h, 8, "q", 0, qT, 0)
                    split_next(l, phase, h, 0)
                    qkv(l, phase, h, 9, "k", 0, kT, 1)
                    split_next(l, phase, h, 1)
                    assemble(l, phase, h)

            def split_merged(l, m):
                act.wait_ge(mix_done.sem, mix_done.after(l, "AMIX", 0, m + 1))
                act.activation(xh[:, m, :], stream[:, m, :], ACT.Copy, scale=0.5).then_inc(mh_ready.sem, 1)

            def square_new(l, phase, i, p, n):
                act.wait_ge(pair_free[p].sem, pair_free[p].after(l, phase, i, 1))
                act.wait_ge(sumsq_step.sem, sumsq_step.after(l, phase, i, p - 1))
                square(tile_of(stream, n), p, sq_ready, n)

            for n in range(KT):
                act.wait_ge(x_in[n], 16)
                if n >= 2:
                    act.wait_ge(sumsq_step.sem, n)
                square(stream[:, n, :], n % 2, sq_ready, n)
            act.wait_ge(const_in, 48)

            with act.Fori(0, DEPTH) as l:
                split_hi(l, "PRE", 0, 0)
                split_hi(l, "PRE", 0, 1)
                normalise(l)
                act.wait_ge(par_step.sem, par_step.after(l, "PRE", 0, 3))
                act.activation(lam_t[:, 1, :], lam_t[:, 0, :], ACT.Exp, scale=-1.0).then_inc(lam_exp.sem, 1)
                act.wait_ge(par_step.sem, par_step.after(l, "PRE", 0, 20))
                for t in range(2):
                    job(l, "PRE", 0, t + 1)
                    start_conv(l, "PRE", 0, 0, t)
                    split_hi(l, "LRU", 0, t)
                    split_xc(l, "PRE", 0, 0, t, (2, 1)[t])
                act.wait_ge(x_kept.sem, x_kept.after(l, "PRE", 0, KT))
                with act.Fori(0, 3) as b:
                    lru(l, "LRU", b, b, False)
                lru(l, "LRUL", 0, 3, True)
                with act.Fori(0, 3) as i:
                    mix(l, "LMIX", i, 1)
                for p in range(2):
                    job(l, "LMIXL", 0, p + 1)
                    split_hi(l, "QK", 0, p)
                for p, (which, to) in enumerate((("q", qT), ("k", kT))):
                    qkv(l, "QK", 0, p, which, 0, to, p)
                    split_hi(l, "ATT", 0, p)
                with act.Fori(0, 3) as h:
                    attention(l, "ATT", h, False)
                attention(l, "ATTL", 0, True)
                with act.Fori(0, 3) as i:
                    mix(l, "AMIX", i, 0)
                for p in range(2):
                    for m in range(3 * p, 3 * p + 3):
                        split_merged(l, m)
                    job(l, "AMIXL", 0, p + 1)
                    split_hi(l, "WOUT", 0, p)
                split_merged(l, 6)
                split_merged(l, 7)
                with act.Fori(0, 3) as i:
                    for p in range(2):
                        job(l, "WOUT", i, p + 1)
                        split_next(l, "WOUT", i, p)
                        square_new(l, "WOUT", i, p, i * 2 + p)
                for p in range(2):
                    square_new(l, "WOUTL", 0, p, KT - 2 + p)
            normalise(DEPTH, final=True)

        @block.gpsimd
        def _(pool):
            pool.memset(eps[:], EPS).then_inc(w_lo.sem, 1)
            pool.memset(ones[:], 1.0).then_inc(w_lo.sem, 1)
            pool.memset(negmax[:], 0.0).then_inc(started, 1)

            def low(to, full, high, signal):
                pool.tensor_tensor(to, full, high.bitcast(F32), ALU.subtract).then_inc(signal.sem, 1)

            def split_lo(l, phase, i, k, width=KT * P):
                pool.wait_ge(w_hi.sem, w_hi.after(l, phase, i, k + 1))
                low(wl[:, k % 2, 0:width], raw[:, k % 2, 0:width], wh[:, k % 2, 0:width], w_lo)

            def split_next(l, phase, i, k, width=KT * P):
                pool.wait_ge(w_hi.sem, w_hi.after(l, phase, i + 1, k + 1))
                low(wl[:, k % 2, 0:width], raw[:, k % 2, 0:width], wh[:, k % 2, 0:width], w_lo)

            def low_xc(l, phase, i, b, t):
                pool.wait_ge(xc_hi.sem, xc_hi.after(l, phase, i, t + 1))
                low(tile_of(yl, b * TPB + t), xc[:, t, :], tile_of(yh, b * TPB + t), xc_lo)

            def low_y(l, phase, i, b, t):
                pool.wait_ge(y_hi.sem, y_hi.after(l, phase, i, t + 1))
                low(tile_of(yl, b * TPB + t), hsum[:, t, :], tile_of(yh, b * TPB + t), y_lo)

            def lru(l, phase, i, b, last):
                for k in range(2, 6):
                    split_lo(l, phase, i, k)
                for t in range(2):
                    if last:
                        split_lo(l, "LMIX", 0, t)
                    else:
                        split_next(l, phase, i, t)
                        low_xc(l, phase, i, b + 1, t)
                for t in range(2):
                    low_y(l, phase, i, b, t)

            def clear_sum(value):
                pool.memset(sumsq[:], 0.0).then_inc(sumsq_step.sem, 1)
                pool.wait_ge(sumsq_step.sem, value)

            def add_square(p, have, prior):
                pool.wait_ge(sq_ready.sem, have)
                pool.wait_ge(sumsq_step.sem, prior)
                pool.tensor_tensor(sumsq[:], sumsq[:], sq[:, p, :], ALU.add).then_inc(sumsq_step.sem, 1)

            clear_sum(1)
            for n in range(KT):
                add_square(n % 2, n + 1, n + 1)

            with pool.Fori(0, DEPTH) as l:
                split_lo(l, "PRE", 0, 0)
                split_lo(l, "PRE", 0, 1)
                for k in range(1, KT, 2):
                    pool.wait_ge(xh_ready.sem, xh_ready.after(l, "PRE", 0, k + 1))
                    low(xl[:, k, :], xf[:, 1, :], xh[:, k, :], xl_pool)
                for t in range(2):
                    split_lo(l, "LRU", 0, t)
                    low_xc(l, "PRE", 0, 0, t)
                with pool.Fori(0, 3) as b:
                    lru(l, "LRU", b, b, False)
                lru(l, "LRUL", 0, 3, True)
                with pool.Fori(0, 3) as i:
                    for k in (2, 3):
                        split_lo(l, "LMIX", i, k)
                    for k in (0, 1):
                        split_next(l, "LMIX", i, k)
                for phase in ("QK", "ATT"):
                    for k in (0, 1):
                        split_lo(l, phase, 0, k)
                with pool.Fori(0, 3) as h:
                    for k in range(2, 10):
                        split_lo(l, "ATT", h, k)
                    for k in (0, 1):
                        split_next(l, "ATT", h, k)
                for k in range(2, 10):
                    split_lo(l, "ATTL", 0, k)
                for k in (0, 1):
                    split_lo(l, "AMIX", 0, k, ATT_OUT)
                with pool.Fori(0, 3) as i:
                    for k in (2, 3):
                        split_lo(l, "AMIX", i, k)
                    for k in (0, 1):
                        split_next(l, "AMIX", i, k, ATT_OUT)
                hold(pool, mix_done.sem, mix_done.after(l, "AMIXL", 0, 1))
                clear_sum(sumsq_step.after(l, "AMIXL", 0, 1))
                for k in (0, 1):
                    split_lo(l, "WOUT", 0, k)
                with pool.Fori(0, 3) as i:
                    for p in range(2):
                        split_next(l, "WOUT", i, p)
                        add_square(p, sq_ready.after(l, "WOUT", i, p + 1), sumsq_step.after(l, "WOUT", i, p))
                for p in range(2):
                    add_square(p, sq_ready.after(l, "WOUTL", 0, p + 1), sumsq_step.after(l, "WOUTL", 0, p))

        @block.vector
        def _(dve):
            for n, s in enumerate([pair_free[0], pair_free[1], pair_free[2], pair_free[3], bank_free[0], bank_free[1],
                                   y_lo, asm_step]):
                dve.memset(rowmax[:, n:n + 1], 0.0).then_inc(s.sem, 1)
            dve.wait_ge(const_in, 48)

            def normalise(l, final=False):
                dve.wait_ge(pair_free[0].sem, pair_free[0].after(l, "PRE", 0, 1))
                dve.reciprocal(rinv[:], rms[:]).then_inc(norm_step.sem, 1)
                dve.wait_ge(norm_step.sem, norm_step.after(l, "PRE", 0, 1))
                dve.tensor_tensor(diag[:], ident[:].unsqueeze(1).broadcast_to([P, KT, P]),
                                  rinv[:].unsqueeze(2).broadcast_to([P, KT, P]), ALU.mult).then_inc(norm_step.sem, 1)
                dve.wait_ge(norm_done.sem, norm_done.after(l, "PRE", 0, 2))
                if final:
                    for k in range(KT):
                        dve.scalar_tensor_tensor(out=stream[:, k, :], in0=stream[:, k, :], scalar=gfin[:, k:k + 1],
                                                 in1=pair[1][:], op0=ALU.mult, op1=ALU.mult).then_inc(fin_ready, 1)
                    return
                dve.wait_ge(par_step.sem, par_step.after(l, "PRE", 0, 1))
                for k in range(KT + 1):
                    if k < KT:
                        if k == 3 or k == 5 or k == 7:
                            dve.wait_ge(xl_pool.sem, xl_pool.after(l, "PRE", 0, k // 2))
                        elif k % 2 == 0 and k:
                            dve.wait_ge(xl_dve.sem, xl_dve.after(l, "PRE", 0, k // 2))
                        dve.scalar_tensor_tensor(out=xf[:, k % 2, :], in0=stream[:, k, :],
                                                 scalar=par[:, PAR_NORM + k:PAR_NORM + k + 1], in1=pair[1][:],
                                                 op0=ALU.mult, op1=ALU.mult).then_inc(xf_ready.sem, 1)
                    if k % 2 == 1:
                        dve.wait_ge(xh_ready.sem, xh_ready.after(l, "PRE", 0, k))
                        dve.tensor_tensor(xl[:, k - 1, :], xf[:, 0, :], xh[:, k - 1, :].bitcast(F32), ALU.subtract)\
                            .then_inc(xl_dve.sem, 1)

            def prepare(l):
                n = [1]

                def step(instruction):
                    instruction.then_inc(par_step.sem, 1)
                    n[0] += 1
                    dve.wait_ge(par_step.sem, par_step.after(l, "PRE", 0, n[0]))

                lam = par[:, PAR_LAM:PAR_LAM + 2 * KT]
                step(dve.tensor_scalar(half[:], par[:, PAR_GATE:PAR_GATE + N_HALF], 0.5, None, ALU.mult))
                step(dve.scalar_tensor_tensor(out=lam_t[:, 0, :], in0=lam, scalar=-1.0, in1=lam, op0=ALU.mult,
                                              op1=ALU.max))
                step(dve.tensor_scalar(lam_t[:, 5, :], lam, -1.0, 0.0, ALU.mult, ALU.max))
                dve.wait_ge(lam_exp.sem, lam_exp.after(l, "PRE", 0, 1))
                step(dve.tensor_scalar(lam_t[:, 2, :], lam_t[:, 1, :], 2.0, None, ALU.add))
                step(dve.reciprocal(lam_t[:, 3, :], lam_t[:, 2, :]))
                step(dve.tensor_tensor(lam_t[:, 2, :], lam_t[:, 3, :], lam_t[:, 1, :], ALU.mult))
                step(dve.tensor_tensor(lam_t[:, 3, :], lam_t[:, 2, :], lam_t[:, 2, :], ALU.mult))
                step(dve.tensor_scalar(lam_t[:, 4, :], lam_t[:, 3, :], 1.0 / 17, None, ALU.mult))
                for odd in range(15, 1, -2):
                    step(dve.scalar_tensor_tensor(out=lam_t[:, 4, :], in0=lam_t[:, 4, :], scalar=1.0 / odd,
                                                  in1=lam_t[:, 3, :], op0=ALU.add, op1=ALU.mult))
                step(dve.scalar_tensor_tensor(out=lam_t[:, 4, :], in0=lam_t[:, 4, :], scalar=1.0, in1=lam_t[:, 2, :],
                                              op0=ALU.add, op1=ALU.mult))
                step(dve.scalar_tensor_tensor(out=lam_t[:, 3, :], in0=lam_t[:, 4, :], scalar=2.0, in1=lam_t[:, 5, :],
                                              op0=ALU.mult, op1=ALU.add))
                step(dve.tensor_scalar(decay_k[:], lam_t[:, 3, :], -4.0, None, ALU.mult))
                step(dve.tensor_scalar(half_k[:], lam_t[:, 3, :], 2.0, None, ALU.mult))
                assert n[0] == 20

            def conv(l, phase, i, b, t):
                c = b * TPB + t
                dve.wait_ge(conv_init.sem, conv_init.after(l, phase, i, t + 1))
                for n, tap in enumerate((0, 1, 3)):
                    shift = tap - 2
                    lo, hi = max(0, -shift), SEQ - max(0, shift)
                    if n:
                        dve.wait_ge(conv_step.sem, conv_step.after(l, phase, i, 2 * t + n))
                    dve.scalar_tensor_tensor(out=xc[:, t, lo:hi], in0=pair[t][:, lo + shift:hi + shift],
                                             scalar=col(par, c + (PAR_CONV + tap * KT)), in1=xc[:, t, lo:hi],
                                             op0=ALU.mult, op1=ALU.add)\
                        .then_inc((conv_step, conv_step, pair_free[t])[n].sem, 1)

            def lru(l, phase, i, b, last):
                def after(k):
                    dve.wait_ge(rec_step.sem, rec_step.after(l, phase, i, k))

                for t in range(2):
                    dve.wait_ge(silu_tanh.sem, silu_tanh.after(l, phase, i, t + 1))
                    dve.scalar_tensor_tensor(out=silu[:, t, :], in0=silu[:, t, :], scalar=1.0, in1=pair[t][:],
                                             op0=ALU.add, op1=ALU.mult).then_inc(pair_free[t].sem, 1)
                for d in range(2):
                    for t in range(2):
                        o = d * 4 + t * 2 + 1
                        q = (2 + o) % 4
                        dve.wait_ge(pair_free[q].sem, pair_free[q].after(l, phase, i, RG_FREES[o]))
                        gated = (gated0, gated1)[d]
                        dve.scalar_tensor_tensor(out=gated[:, t, :], in0=gated[:, t, :], scalar=1.0, in1=xc[:, t, :],
                                                 op0=ALU.add, op1=ALU.mult).then_inc(rec_step.sem, 1)
                for d in range(2):
                    gated, root = (gated0, gated1)[d], (root0, root1)[d]
                    s = 5 + 6 * d
                    inner = slice(1, SEQ) if d == 0 else slice(0, SEQ - 1)
                    for t in range(2):
                        dve.wait_ge(decay_ready.sem, decay_ready.after(l, phase, i, 2 * d + t + 1))
                        after(1 + 2 * d + t)
                        dve.scalar_tensor_tensor(out=gated[:, t, inner], in0=decay[:, t, inner], scalar=1.0,
                                                 in1=gated[:, t, inner], op0=ALU.add, op1=ALU.mult)\
                            .then_inc(rec_step.sem, 1)
                    for t in range(2):
                        dve.wait_ge(root_ready.sem, root_ready.after(l, phase, i, 2 * d + t + 1))
                        after(s + t)
                        dve.tensor_tensor(gated[:, t, inner], gated[:, t, inner], root[:, t, inner], ALU.mult)\
                            .then_inc(rec_step.sem, 1)
                    for t in range(2):
                        after(s + 2 + t)
                        if d == 0:
                            if t == 0:
                                dve.wait_ge(y_lo.sem, y_lo.after(l, phase, i, 0))
                            dve.tensor_tensor_scan(hsum[:, t, :], decay[:, t, :], gated[:, t, :], 0.0, op0=ALU.mult,
                                                   op1=ALU.add).then_inc(rec_step.sem, 1)
                        else:
                            dve.tensor_tensor_scan(root[:, t, ::-1], decay[:, t, ::-1], gated[:, t, ::-1], 0.0,
                                                   op0=ALU.mult, op1=ALU.add).then_inc(rec_step.sem, 1)
                    if not last:
                        conv(l, phase, i, b + 1, d)
                for t in range(2):
                    after(15 + t)
                    dve.tensor_tensor(hsum[:, t, :], hsum[:, t, :], root1[:, t, :], ALU.add).then_inc(rec_step.sem, 1)
                    after(17 + 2 * t)
                    dve.scalar_tensor_tensor(out=hsum[:, t, :], in0=hsum[:, t, :], scalar=0.25, in1=silu[:, t, :],
                                             op0=ALU.mult, op1=ALU.mult).then_inc(rec_step.sem, 1)

            def mix(l, phase, i, branch, p, m, gate_free):
                dve.wait_ge(job_done.sem, job_done.after(l, phase, i, p + 1))
                dve.wait_ge(pair_free[p].sem, gate_free)
                out = tile_of(stream, m) if branch else gate[:, p, :]
                dve.scalar_tensor_tensor(out=out, in0=gate[:, p, :], scalar=1.0, in1=pair[p][:], op0=ALU.add,
                                         op1=ALU.mult).then_inc(pair_free[p].sem, 1)
                if not branch:
                    dve.wait_ge(pair_free[p].sem, pair_free[p].after(l, phase, i, 1))
                    dve.tensor_tensor(tile_of(stream, m), tile_of(stream, m), gate[:, p, :], ALU.add)\
                        .then_inc(mix_done.sem, 1)

            def score_rows(l, phase, h, g):
                for n, u in enumerate(UNITS_OF[g]):
                    use = SCORES_AT[g] + n
                    hold(dve, unit_ready.sem, unit_ready.after(l, phase, h, use + 1))
                    for _, kind, idx, column, width, stat in UNITS[u]:
                        at_bias = BIAS_AT[g, kind]
                        e = dve.tensor_tensor_reduce(
                            scores[:, u, column:column + width], bank[use % 2][:, column:column + width],
                            bias[:, at_bias:at_bias + width], 1.0, -3e38, ALU.add, ALU.max, rowmax[:, stat:stat + 1])
                    e.then_inc(bank_free[use % 2].sem, 1)

            def combine(arrived, steps, l, phase, h, op):
                dve.wait_ge(arrived.sem, arrived.after(l, phase, h, 1))
                dve.tensor_tensor(stat_t[:, 0, :], stat_c[:, 0, :], stat_c[:, 1, :], op).then_inc(steps.sem, 1)
                dve.wait_ge(steps.sem, steps.after(l, phase, h, 1))
                dve.tensor_tensor(stat_t[:, 1, :], stat_t[:, 0, :], stat_c[:, 2, :], op).then_inc(steps.sem, 1)
                dve.wait_ge(steps.sem, steps.after(l, phase, h, 2))
                if op == ALU.max:
                    dve.tensor_scalar(stat_t[:, 2, :], stat_t[:, 1, :], -1.0, None, ALU.mult).then_inc(steps.sem, 1)
                else:
                    dve.reciprocal(stat_t[:, 2, :], stat_t[:, 1, :]).then_inc(steps.sem, 1)

            def attention(l, phase, h, last):
                dve.wait_ge(bias_in.sem, bias_in.after(l, phase, h, 0))
                for g in range(N_GROUPS):
                    score_rows(l, phase, h, g)
                combine(max_in, max_step, l, phase, h, ALU.max)
                dve.wait_ge(silu_tanh.sem, silu_tanh.after(l, phase, h, 1))
                dve.scalar_tensor_tensor(out=silu_a[:], in0=silu_a[:], scalar=1.0, in1=pair[1][:], op0=ALU.add,
                                         op1=ALU.mult).then_inc(pair_free[1].sem, 1)
                if not last:
                    combine(den_in, den_step, l, phase, h, ALU.add)
                for u in range(N_UNITS):
                    use = PT_AT + u
                    width = sum(t[4] for t in UNITS[u])
                    dve.wait_ge(unit_ready.sem, unit_ready.after(l, phase, h, use + 1))
                    dve.tensor_copy(pT[:, u % 3, 0:width], bank[use % 2][:, 0:width]).then_inc(bank_free[use % 2].sem, 1)
                dve.wait_ge(pair_free[3].sem, pair_free[3].after(l, phase, h, 1))
                dve.wait_ge(asm_start.sem, asm_start.after(l, phase, h, 1))
                dve.wait_ge(pv_done.sem, pv_done.after(l, phase, h, 2))
                ordered = in_group(1, pair[1][:])
                late, early = by_group(1, acc[:, 256:SEQ]), by_group(1, acc[:, 0:256])
                dve.tensor_tensor(late, late, ordered[:, :, 0:192], ALU.add).then_inc(asm_step.sem, 1)
                dve.tensor_tensor(early, early, ordered[:, :, 192:256], ALU.add).then_inc(pair_free[1].sem, 1)
                pv_free = 5 if last else 6
                dve.wait_ge(asm_step.sem, asm_step.after(l, phase, h, 1))
                dve.wait_ge(pair_free[1].sem, pair_free[1].after(l, phase, h, pv_free))
                dve.wait_ge(pv_done.sem, pv_done.after(l, phase, h, 3))
                token = by_group(2, acc[:])
                dve.tensor_tensor(token, token, in_group(2, pair[3][:]), ALU.add).then_inc(pair_free[3].sem, 1)
                if last:
                    combine(den_in, den_step, l, phase, h, ALU.add)
                dve.wait_ge(pair_free[3].sem, pair_free[3].after(l, phase, h, 2))
                dve.wait_ge(rden_in.sem, rden_in.after(l, phase, h, 1))
                dve.tensor_tensor(acc[:], acc[:], rden[:], ALU.mult).then_inc(asm_step.sem, 1)
                dve.wait_ge(asm_step.sem, asm_step.after(l, phase, h, 2))
                dve.tensor_tensor(acc[:], acc[:], silu_a[:], ALU.mult).then_inc(asm_step.sem, 1)
                dve.wait_ge(ya_hi.sem, ya_hi.after(l, phase, h, 1))
                slot = HEADS_PER_GROUP - 1 if last else h
                dve.scalar_tensor_tensor(out=tile_of(yal, slot), in0=acc[:], scalar=0.5,
                                         in1=tile_of(yah, slot).bitcast(F32), op0=ALU.mult, op1=ALU.subtract)\
                    .then_inc(ya_lo.sem, 1)

            def split_merged(l, m):
                dve.wait_ge(mh_ready.sem, mh_ready.after(l, "AMIXL", 0, m + 1))
                dve.scalar_tensor_tensor(out=xl[:, m, :], in0=stream[:, m, :], scalar=0.5,
                                         in1=xh[:, m, :].bitcast(F32), op0=ALU.mult, op1=ALU.subtract)\
                    .then_inc(ml_ready.sem, 1)

            def add_residual(l, phase, i, p, n):
                dve.wait_ge(job_done.sem, job_done.after(l, phase, i, p + 1))
                dve.wait_ge(xold_in[p].sem, xold_in[p].after(l, phase, i, 1))
                dve.tensor_tensor(tile_of(stream, n), xold[:, p, :], pair[p][:], ALU.add)\
                    .then_inc(pair_free[p].sem, 1)

            with dve.Fori(0, DEPTH) as l:
                dve.tensor_copy(par[:], tile_of(par_all, l)).then_inc(par_step.sem, 1)
                normalise(l)
                prepare(l)
                for t in range(2):
                    conv(l, "PRE", 0, 0, t)
                with dve.Fori(0, 3) as b:
                    lru(l, "LRU", b, b, False)
                lru(l, "LRUL", 0, 3, True)
                with dve.Fori(0, 3) as i:
                    for p in range(2):
                        mix(l, "LMIX", i, 1, p, i * 2 + p, pair_free[p].after(l, "LMIX", i, 0))
                for p in range(2):
                    mix(l, "LMIXL", 0, 1, p, KT - 2 + p, pair_free[p].after(l, "LMIXL", 0, 0))
                with dve.Fori(0, 3) as h:
                    attention(l, "ATT", h, False)
                attention(l, "ATTL", 0, True)
                with dve.Fori(0, 3) as i:
                    for p in range(2):
                        mix(l, "AMIX", i, 0, p, i * 2 + p, pair_free[p].after(l, "AMIX", i, 0))
                for p in range(2):
                    for m in range(3 * p, 3 * p + 3):
                        split_merged(l, m)
                    mix(l, "AMIXL", 0, 0, p, KT - 2 + p, pair_free[p].after(l, "AMIXL", 0, 0))
                split_merged(l, 6)
                split_merged(l, 7)
                with dve.Fori(0, 3) as i:
                    for p in range(2):
                        add_residual(l, "WOUT", i, p, i * 2 + p)
                for p in range(2):
                    add_residual(l, "WOUTL", 0, p, KT - 2 + p)
            normalise(DEPTH, final=True)

        @block.tensor
        def _(pe):
            def product(out, k, high, low, ks, begin=True, end=True, ready=None):
                for n in ks:
                    if ready:
                        ready(n)
                    columns = slice(n * P, (n + 1) * P)
                    for w, x, first, final in ((wh, high, True, False), (wh, low, False, False), (wl, high, False, True)):
                        for s in range(2):
                            token = slice(s * HALF, (s + 1) * HALF)
                            e = pe.matmul(out[:, token], w[:, k % 2, columns], x[:, n, token],
                                          start=begin and first and n == ks[0],
                                          stop=end and final and n == ks[-1])
                return e

            def dense(l, phase, i, k, use, high=xh, low=xl, tiles=KT, done=None, ready=None):
                pe.wait_ge(w_lo.sem, w_lo.after(l, phase, i, k + 1))
                q = pair_free[k % 2]
                pe.wait_ge(q.sem, q.after(l, phase, i, use))
                product(pair[k % 2], k, high, low, range(tiles), ready=ready).then_inc(job_done.sem, 1)

            def normalise(l):
                pe.wait_ge(sumsq_step.sem, sumsq_step.after(l, "PRE", 0, 0))
                pe.wait_ge(pair_free[0].sem, pair_free[0].after(l, "PRE", 0, 0))
                for n in range(KT):
                    e = pe.matmul(pair[0][:, n:n + 1], sumsq[:, n * P:(n + 1) * P], ones[:, 0:1], start=True, stop=True)
                e.then_inc(norm_done.sem, 1)
                pe.wait_ge(norm_step.sem, norm_step.after(l, "PRE", 0, 2))
                pe.wait_ge(pair_free[1].sem, pair_free[1].after(l, "PRE", 0, 0))
                for n in range(KT):
                    e = pe.matmul(pair[1][:, n * P:(n + 1) * P], ones[:], diag[:, n, :], start=True, stop=True)
                e.then_inc(norm_done.sem, 1)

            def rg(l, phase, i, b, d):
                k = 2 + d
                pe.wait_ge(w_lo.sem, w_lo.after(l, phase, i, k + 1))
                for t in range(2):
                    for which in range(2):
                        o = d * 4 + t * 2 + which
                        q = pair_free[(2 + o) % 4]
                        pe.wait_ge(q.sem, q.after(l, phase, i, RG_FREES[o] - 1))
                        for n in range(TPB):
                            at_w = which * 2 * BLOCK_W + n * BLOCK_W + t * P
                            for w, x, first, final in ((wh, yh, True, False), (wh, yl, False, False),
                                                       (wl, yh, False, True)):
                                for s in range(2):
                                    token = slice(s * HALF, (s + 1) * HALF)
                                    if isinstance(b, int):
                                        moving = x[:, b * TPB + n, token]
                                    else:
                                        moving = x[:, bass.ds(b * TPB + n, 1), token].rearrange("p a s -> p (a s)")
                                    e = pe.matmul(pair[(2 + o) % 4][:, token], w[:, k % 2, at_w:at_w + P], moving,
                                                  start=first and n == 0, stop=final and n == TPB - 1)
                        e.then_inc(rg_done.sem, 1)

            def lru(l, phase, i, b, last):
                for k in range(2):
                    dense(l, phase, i, k, 0)
                if last:
                    pe.wait_ge(xc_lo.sem, xc_lo.after(l, "LRUL", 0, 0))
                else:
                    pe.wait_ge(xc_lo.sem, xc_lo.after(l, phase, i, 0))
                if last or isinstance(b, int):
                    pass
                for n in range(2):
                    pe.wait_ge(bank_free[n].sem, bank_free[n].after(l, "PRE", 0, 0))
                rg(l, phase, i, b, 0)
                rg(l, phase, i, b, 1)
                for k in range(2):
                    dense(l, phase, i, 4 + k, 3)

            def bank_use(l, phase, h, use):
                b = bank_free[use % 2]
                pe.wait_ge(b.sem, b.after(l, phase, h, use // 2))

            def score(l, phase, h, g):
                for n, u in enumerate(UNITS_OF[g]):
                    use = SCORES_AT[g] + n
                    bank_use(l, phase, h, use)
                    for _, kind, idx, column, width, stat in UNITS[u]:
                        out = bank[use % 2][:, column:column + width]
                        length = SEQ // DILATION[g]
                        if kind == "mid":
                            key = idx * P if g == 0 else idx * length
                            e = pe.matmul(out, qT[:, key + 64:key + 64 + P], kT[:, key:key + 2 * P], start=True, stop=True)
                        elif kind == "full":
                            e = pe.matmul(out, qT[:, idx * P:(idx + 1) * P], kT[:, idx * P:(idx + 1) * P],
                                          start=True, stop=True)
                        else:
                            first, end = idx * length, (idx + 1) * length
                            pe.matmul(out[0:64, :], qT[:, end - 64:end], kT[:, end - P:end], start=True, stop=True)
                            e = pe.matmul(out[64:128, :], qT[:, first:first + 64], kT[:, first:first + P],
                                          start=True, stop=True)
                    e.then_inc(unit_ready.sem, 1)

            def turn_values(l, phase, h, g):
                for n in range(2):
                    use = VT_AT[g] + n
                    bank_use(l, phase, h, use)
                    for c in range(4):
                        e = pe.transpose(bank[use % 2][:, c * P:(c + 1) * P],
                                         vT[:, (4 * n + c) * P:(4 * n + c + 1) * P], ident[:])
                    e.then_inc(unit_ready.sem, 1)

            def turn_probs(l, phase, h, u):
                use = PT_AT + u
                bank_use(l, phase, h, use)
                pe.wait_ge(exp_done.sem, exp_done.after(l, phase, h, u + 1))
                width = sum(t[4] for t in UNITS[u])
                for c in range(width // P):
                    e = pe.transpose(bank[use % 2][:, c * P:(c + 1) * P], scores[:, u, c * P:(c + 1) * P], ident[:])
                e.then_inc(unit_ready.sem, 1)

            def numerators(l, phase, h, u, last):
                use = PT_AT + u
                b = bank_free[use % 2]
                pe.wait_ge(b.sem, b.after(l, phase, h, use // 2 + 1))
                g = UNITS[u][0][0]
                out = pair[(3, 1, 3)[g]]
                if u == UNITS_OF[g][0]:
                    if g == 1:
                        pe.wait_ge(pair_free[1].sem, pair_free[1].after(l, phase, h, 4 if last else 5))
                    else:
                        pe.wait_ge(pair_free[3].sem, pair_free[3].after(l, phase, h, g // 2))
                prob = pT[:, u % 3, :]
                for _, kind, idx, column, width, stat in UNITS[u]:
                    chunks = SEQ // DILATION[g] // P
                    if kind == "mid":
                        at_out = idx * P if g == 0 else idx * 2 * P
                        chunk = idx if g == 0 else 2 * idx
                        for c in range(2):
                            e = pe.matmul(out[:, at_out:at_out + P], values[:, g, chunk + c, :],
                                          prob[:, column + c * P:column + (c + 1) * P], start=c == 0, stop=c == 1)
                    elif kind == "full":
                        e = pe.matmul(out[:, idx * P:(idx + 1) * P], values[:, g, idx, :],
                                      prob[:, column:column + P], start=True, stop=True)
                    else:
                        at_out = (idx + 1) * chunks * P - P
                        for c, chunk in ((0, (idx + 1) * chunks - 1), (1, idx * chunks)):
                            e = pe.matmul(out[:, at_out + 64 * c:at_out + 64 * c + 64], values[:, g, chunk, :],
                                          prob[:, column + 64 * c:column + 64 * c + 64], start=True, stop=True)
                if u == UNITS_OF[g][-1]:
                    e.then_inc(pv_done.sem, 1)

            def output(l, phase, h, last):
                turn_probs(l, phase, h, 0)
                for u in range(1, N_UNITS):
                    turn_probs(l, phase, h, u)
                    numerators(l, phase, h, u - 1, last)
                numerators(l, phase, h, N_UNITS - 1, last)

            def attention(l, phase, h, last):
                def have(p, n):
                    pe.wait_ge(pair_free[p].sem, pair_free[p].after(l, phase, h, n))

                dense(l, phase, h, 0, 0)
                have(0, 0)
                have(1, 0)
                score(l, phase, h, 0)
                dense(l, phase, h, 1, 0)
                have(0, 1)
                turn_values(l, phase, h, 0)
                dense(l, phase, h, 2, 1)
                dense(l, phase, h, 3, 1)
                have(0, 2)
                score(l, phase, h, 1)
                dense(l, phase, h, 4, 2)
                have(1, 2)
                turn_values(l, phase, h, 1)
                dense(l, phase, h, 5, 2)
                dense(l, phase, h, 6, 3)
                have(1, 3)
                score(l, phase, h, 2)
                dense(l, phase, h, 7, 3)
                have(0, 4)
                turn_values(l, phase, h, 2)
                dense(l, phase, h, 8, 4)
                if last:
                    output(l, phase, h, last)
                    dense(l, phase, h, 9, 5)
                else:
                    dense(l, phase, h, 9, 4)
                    output(l, phase, h, last)

            with pe.Fori(0, DEPTH) as l:
                normalise(l)

                def xn_ready(n):
                    s = (xl_dve, xl_pool)[n % 2]
                    pe.wait_ge(s.sem, s.after(l, "PRE", 0, n // 2 + 1))

                dense(l, "PRE", 0, 0, 1, ready=xn_ready)
                dense(l, "PRE", 0, 1, 0)
                with pe.Fori(0, 3) as b:
                    lru(l, "LRU", b, b, False)
                lru(l, "LRUL", 0, 3, True)
                hold(pe, y_lo.sem, y_lo.after(l, "LMIX", 0, 0))
                with pe.Fori(0, 3) as i:
                    for k in range(2):
                        dense(l, "LMIX", i, k, 0, yh, yl)
                    for k in range(2, 4):
                        dense(l, "LMIX", i, k, 1)
                for k in range(2):
                    dense(l, "LMIXL", 0, k, 0, yh, yl)
                for k in range(2):
                    dense(l, "QK", 0, k, 0)
                hold(pe, pair_free[2].sem, pair_free[2].after(l, "QK", 0, 0))
                with pe.Fori(0, 3) as h:
                    attention(l, "ATT", h, False)
                attention(l, "ATTL", 0, True)
                hold(pe, ya_lo.sem, ya_lo.after(l, "AMIX", 0, 0))
                with pe.Fori(0, 3) as i:
                    for k in range(2):
                        dense(l, "AMIX", i, k, 0, yah, yal, ATT_KT)
                    for k in range(2, 4):
                        dense(l, "AMIX", i, k, 1)
                for k in range(2):
                    dense(l, "AMIXL", 0, k, 0, yah, yal, ATT_KT)

                def merged_ready(n):
                    pe.wait_ge(ml_ready.sem, ml_ready.after(l, "AMIXL", 0, n + 1))

                with pe.Fori(0, 3) as i:
                    for k in range(2):
                        dense(l, "WOUT", i, k, 0, ready=merged_ready if k == 0 else None)
                for k in range(2):
                    dense(l, "WOUTL", 0, k, 0)
            normalise(DEPTH)


def _starts(per):
    start, total = {}, 0
    for name, times in PHASES:
        start[name] = total
        total += per[name] * times
    return start


JOBS_START = _starts(JOBS)
RG_FREES = [1, 1, 2, 2, 2, 2, 3, 3]
PAIR_LRU = [4, 4]


def _block(w):
    k, n = w.shape
    return w.reshape(k // P, P, n).transpose(1, 0, 2).reshape(P, k // P * n)


def _columns(v):
    return v.reshape(-1, KT, P).transpose(2, 0, 1).reshape(P, -1)


def _bias_tables():
    n_heads = N_GROUPS * HEADS_PER_GROUP
    slopes = np.float32(2.0) ** (np.float32(-8.0) * np.arange(1, n_heads + 1, dtype=np.float32) / np.float32(n_heads))
    row, key = np.arange(P)[:, None], np.arange(2 * P)[None, :]
    mid = key - (row + 64)
    edge = key[:, :P] - np.where(row < 64, row + 64, row - 64)
    full = np.where(row // 64 == key[:, :P] // 64, key[:, :P] - row, 10 * P)
    table = np.zeros((HEADS_PER_GROUP, P, N_BIAS), np.float32)
    for (g, kind), at in BIAS_AT.items():
        delta = np.abs({"mid": mid, "edge": edge, "full": full}[kind])
        for h in range(HEADS_PER_GROUP):
            bias = -slopes[g * HEADS_PER_GROUP + h] * (delta * DILATION[g]).astype(np.float32)
            table[h, :, at:at + delta.shape[1]] = np.where(delta <= WINDOW_HALF, bias, np.float32(MASKED))
    return table


def kernel(x, norm_g, w_in, b_gate, conv_w, conv_b, rg_w_a, rg_b_a, rg_w_x, rg_b_x, rg_lam, w_o_att, w_o_lru, w_out,
           final_g):
    import concourse.bacc as bacc
    from concourse.bass_utils import run_bass_kernel_spmd

    named = {"w_in": np.asarray(w_in), "w_o_att": np.asarray(w_o_att), "w_o_lru": np.asarray(w_o_lru),
             "w_out": np.asarray(w_out)}
    rg_a, rg_x = np.asarray(rg_w_a), np.asarray(rg_w_x)
    blocks = np.zeros((DEPTH * N_JOBS, P, KT * P), np.float32)
    for l in range(DEPTH):
        for j, what in enumerate(job_columns()):
            if what[0] == "rg":
                _, b, d = what
                blocks[l * N_JOBS + j, :, 0:2 * BLOCK_W] = _block(rg_a[l, d, b])
                blocks[l * N_JOBS + j, :, 2 * BLOCK_W:] = _block(rg_x[l, d, b])
            else:
                part = _block(named[what[0]][l][:, what[1]:what[1] + P])
                blocks[l * N_JOBS + j, :, 0:part.shape[1]] = part
    params = np.stack([np.concatenate([_columns(np.asarray(v)[l]) for v in
                                       (norm_g, conv_w, conv_b, b_gate, rg_b_a, rg_b_x, rg_lam)], axis=1)
                       for l in range(DEPTH)], axis=1)
    arrays = {
        "xT": np.ascontiguousarray(np.asarray(x)[0].T).reshape(KT, P, SEQ),
        "blocks": blocks,
        "params": np.ascontiguousarray(params),
        "final_g": np.ascontiguousarray(_columns(np.asarray(final_g))),
        "bias_table": _bias_tables(),
        "identity": np.eye(P, dtype=np.float32),
    }
    nc = bacc.Bacc("TRN2", target_bir_lowering=False, num_devices=1, dynamic_dma_scratch_size=1024)
    args = [nc.dram_tensor(name, a.shape, mybir.dt.from_np(a.dtype), kind="ExternalInput").ap()
            for name, a in arrays.items()]
    out = nc.dram_tensor("outT", (KT, P, SEQ), F32, kind="ExternalOutput").ap()
    build(nc, *args, out)
    result = run_bass_kernel_spmd(nc, [arrays], core_ids=[0])
    return result.results[0]["outT"].reshape(D_MODEL, SEQ).T.reshape(1, SEQ, D_MODEL)
```

```python
from contextlib import ExitStack

import numpy as np

import concourse.bass as bass
from concourse import mybir

ALU = mybir.AluOpType
ACT = mybir.ActivationFunctionType
F32 = mybir.dt.float32
F32R = mybir.dt.float32r

P = 128
D_MODEL, SEQ, DEPTH = 1024, 1024, 2
KT = D_MODEL // P
HALF = 512
HEADS_PER_GROUP, N_GROUPS, HEAD_DIM = 4, 3, 128
QKV = N_GROUPS * HEADS_PER_GROUP * HEAD_DIM
ATT_OUT = HEADS_PER_GROUP * HEAD_DIM
ATT_KT = ATT_OUT // P
DILATION = (1, 4, 16)
WINDOW_HALF = 64
BLOCKS, BLOCK_W, CONV_W = 4, 256, 4
TPB = BLOCK_W // P
EPS = 1e-6
SCALE = float(HEAD_DIM) ** -0.5
MASKED = -1e30

PAR_CONV, PAR_CONV_B, PAR_GATE, PAR_RGA, PAR_RGX, PAR_LAM, N_PAR = 0, 32, 40, 56, 72, 88, 104
HALF_GATT, HALF_GLRU, HALF_RGA, HALF_RGX, N_HALF = 0, 8, 16, 32, 48

PHASES = (("PRE", 1), ("LRU", 3), ("LRUL", 1), ("LMIX", 2), ("LMIXL", 1), ("QK", 1), ("ATT", 3), ("ATTL", 1),
          ("AMIX", 3), ("AMIXL", 1), ("WOUT", 3), ("WOUTL", 1))


def phases(**n):
    return {name: n.get(name, 0) for name, _ in PHASES}


JOBS = phases(PRE=2, LRU=6, LRUL=8, LMIX=4, LMIXL=4, QK=2, ATT=10, ATTL=10, AMIX=4, AMIXL=2, WOUT=2, WOUTL=2)
N_JOBS = sum(JOBS[name] * times for name, times in PHASES)


class Count:

    def __init__(self, sem, per, head=0, by=1):
        self.sem, self.per, self.head, self.by = sem, per, head, by
        self.start, total = {}, 0
        for name, times in PHASES:
            self.start[name] = total
            total += per[name] * times
        self.layer = total

    def after(self, l, phase, i, k):
        return (l * self.layer + i * self.per[phase] + (self.start[phase] + k)) * self.by + self.head


def units():
    mid0 = [(0, "mid", i, 256, i) for i in range(7)]
    mid1 = [(1, "mid", r, 256, 8 + r) for r in range(4)]
    edge1 = [(1, "edge", r, 128, 12 + r) for r in range(4)]
    full2 = [(2, "full", j, 128, 16 + j) for j in range(8)]
    banks = [[mid0[0], (0, "edge", 0, 128, 7)], mid0[1:3], mid0[3:5], mid0[5:7], mid1[0:2], mid1[2:4], edge1,
             full2[0:4], full2[4:8]]
    out = []
    for tiles in banks:
        column, bank = 0, []
        for g, kind, i, width, stat in tiles:
            bank.append((g, kind, i, column, width, stat))
            column += width
        out.append(bank)
    return out


UNITS = units()
UNITS_OF = [range(0, 4), range(4, 7), range(7, 9)]
N_UNITS = len(UNITS)
N_STATS = 24
SCORES_AT, VT_AT, PT_AT = [0, 6, 11], [4, 9, 13], 15
BANK_USES = PT_AT + N_UNITS
BIAS_AT = {(0, "mid"): 0, (0, "edge"): 256, (1, "mid"): 384, (1, "edge"): 640, (2, "full"): 768}
N_BIAS = 896

ML_POOL = (3, 6)
ML_DVE = tuple(m for m in range(KT) if m not in ML_POOL)
SQUARE_POOL = (3, 6)
SQUARE_ACT = tuple(n for n in range(KT) if n not in SQUARE_POOL)
BLOCK_AFTER = (0, 3)
SPREAD_AT = 3
SCALE_AT = 7


def job_columns():
    x_at, glru_at = 3 * QKV + ATT_OUT, 3 * QKV + ATT_OUT + D_MODEL
    gate_at = glru_at + D_MODEL
    x = lambda b: [("w_in", x_at + (TPB * b + t) * P) for t in range(TPB)]
    gate = lambda which, m: ("w_in", gate_at + which * D_MODEL + m * P)
    qkv = lambda which, g, h: ("w_in", which * QKV + (g * HEADS_PER_GROUP + h) * HEAD_DIM)
    jobs = x(0)
    for b in range(BLOCKS):
        jobs += [("w_in", glru_at + (TPB * b + t) * P) for t in range(TPB)] + [("rg", b, 0), ("rg", b, 1)]
        jobs += x(b + 1) if b + 1 < BLOCKS else [gate(1, m) for m in (2, 3, 4, 5)]
    for outs, gates in (((2, 3), (0, 1)), ((4, 5), (6, 7)), ((0, 1, 6, 7), ())):
        jobs += [("w_o_lru", m * P) for m in outs] + [gate(1, m) for m in gates]
    jobs += [qkv(0, 0, 0), qkv(1, 0, 0)]
    for h in range(HEADS_PER_GROUP):
        jobs += [qkv(2, 0, h)] + [qkv(w, g, h) for g in (1, 2) for w in range(3)] + [("w_in", 3 * QKV + h * HEAD_DIM)]
        jobs += [qkv(0, 0, h + 1), qkv(1, 0, h + 1)] if h + 1 < HEADS_PER_GROUP else [gate(0, 0), gate(0, 1)]
    for i in range(KT // 2):
        jobs += [("w_o_att", (2 * i + t) * P) for t in range(2)]
        jobs += [gate(0, 2 * i + 2), gate(0, 2 * i + 3)] if 2 * i + 2 < KT else []
    return jobs + [("w_out", m * P) for m in range(KT)]


def build(nc, xT, blocks, params, norm_table, bias_table, identity, outT):
    with ExitStack() as ctx:
        def sem(name):
            return ctx.enter_context(nc.semaphore(name))

        def count(name, head=0, by=1, **per):
            return Count(sem(name), phases(**per), head, by)

        half_jobs = {name: n // 2 for name, n in JOBS.items()}
        dense = dict(JOBS, LRU=4, LRUL=6)
        raw_in = [count(f"raw_in{p}", by=16, **half_jobs) for p in range(2)]
        w_hi = count("w_hi", **JOBS)
        w_lo = count("w_lo", head=2, **JOBS)
        job_done = count("job_done", **dense)
        rg_done = count("rg_done", LRU=8, LRUL=8)
        norm_done = count("norm_done", PRE=2)
        x_used = count("x_used", PRE=KT - 1)
        pair_free = [
            count("pair_free0", head=1, PRE=1, LRU=4, LRUL=5, LMIX=2, LMIXL=2, QK=1, ATT=5, ATTL=5, AMIX=2, AMIXL=1,
                  WOUT=1, WOUTL=1),
            count("pair_free1", head=1, PRE=1, LRU=4, LRUL=5, LMIX=2, LMIXL=2, QK=1, ATT=6, ATTL=6, AMIX=2, AMIXL=1,
                  WOUT=1, WOUTL=1),
            count("pair_free2", head=1, PRE=1, LRU=2, LRUL=2),
            count("pair_free3", head=1, PRE=1, LRU=2, LRUL=2, ATT=2, ATTL=2),
        ]
        bank_free = [count(f"bank_free{n}", head=1, ATT=BANK_USES // 2, ATTL=BANK_USES // 2) for n in range(2)]
        x_in = [sem(f"x_in{n}") for n in range(KT)]
        sq_ready = count("sq_ready", head=len(SQUARE_ACT), WOUT=2, WOUTL=2)
        sumsq_step = count("sumsq_step", head=KT + 1, WOUT=2, WOUTL=2, AMIXL=1)
        xg_hi = count("xg_hi", head=KT, WOUT=2, WOUTL=2)
        xg_lo = count("xg_lo", head=KT, WOUT=2, WOUTL=2)
        norm_step = count("norm_step", PRE=2)
        xf_ready = count("xf_ready", PRE=KT)
        xh_ready = count("xh_ready", PRE=KT)
        xl_dve = count("xl_dve", PRE=KT // 2)
        xl_pool = count("xl_pool", PRE=KT // 2)
        sq_pool_ready = sem("sq_pool_ready")
        warmed = count("warmed", head=1, PRE=1)
        fin_ready = sem("fin_ready")
        x_kept = count("x_kept", head=16 * KT, by=16, WOUT=2, WOUTL=2)
        par_step = count("par_step", PRE=20)
        lam_exp = count("lam_exp", PRE=1)
        conv_init = count("conv_init", PRE=2, LRU=2)
        x_scaled = count("x_scaled", PRE=1)
        conv_step = count("conv_step", PRE=6, LRU=4)
        xc_hi = count("xc_hi", PRE=2, LRU=2)
        xc_lo = count("xc_lo", PRE=2, LRU=2)
        silu_tanh = count("silu_tanh", LRU=2, LRUL=2, ATT=1, ATTL=1)
        decay_ready = count("decay_ready", LRU=4, LRUL=4)
        half_decay = count("half_decay", LRU=4, LRUL=4)
        root_ready = count("root_ready", LRU=4, LRUL=4)
        rec_step = count("rec_step", LRU=20, LRUL=20)
        y_hi = count("y_hi", LRU=2, LRUL=2)
        y_lo = count("y_lo", head=1, LRU=2, LRUL=2)
        unit_ready = count("unit_ready", ATT=BANK_USES, ATTL=BANK_USES)
        qkv_ready = count("qkv_ready", QK=2, ATT=9, ATTL=7)
        bias_in = count("bias_in", head=16, by=16, ATT=1, ATTL=1)
        max_out = count("max_out", by=16, ATT=8, ATTL=8)
        max_in = count("max_in", by=16, ATT=1, ATTL=1)
        max_step = count("max_step", ATT=3, ATTL=3)
        negmax_out = count("negmax_out", by=16, ATT=1, ATTL=1)
        negmax_in = [count(f"negmax_in{g}", by=16, ATT=(3, 3, 2)[g], ATTL=(3, 3, 2)[g]) for g in range(N_GROUPS)]
        exp_done = count("exp_done", ATT=N_UNITS, ATTL=N_UNITS)
        den_out = count("den_out", by=16, ATT=8, ATTL=8)
        den_in = count("den_in", by=16, ATT=1, ATTL=1)
        den_step = count("den_step", ATT=3, ATTL=3)
        rden_out = count("rden_out", by=16, ATT=1, ATTL=1)
        rden_in = count("rden_in", by=16, ATT=1, ATTL=1)
        pv_done = count("pv_done", ATT=3, ATTL=3)
        asm_step = count("asm_step", head=1, ATT=3, ATTL=3)
        asm_start = count("asm_start", ATT=1, ATTL=1)
        ya_hi = count("ya_hi", ATT=1, ATTL=1)
        ya_lo = count("ya_lo", ATT=1, ATTL=1)
        mix_done = count("mix_done", AMIX=2, AMIXL=2)
        mh_ready = count("mh_ready", AMIXL=KT)
        ml_dve = count("ml_dve", AMIXL=len(ML_DVE))
        ml_pool = count("ml_pool", AMIXL=len(ML_POOL))
        xold_in = [count(f"xold_in{p}", by=16, WOUT=1, WOUTL=1) for p in range(2)]
        gain_in = sem("gain_in")
        const_in = sem("const_in")
        started = sem("started")
        out_done = sem("out_done")

        KB = 1024
        base = (nc.sbuf_base + 63) // 64 * 64
        at = [base]

        def place(name, shape, dtype=F32, offset=None):
            size = int(np.prod(shape[1:])) * 4
            if offset is None:
                offset = at[0]
                at[0] += (size + 31) // 32 * 32
            assert offset + size <= nc.sbuf_usable_end, (name, offset + size)
            return nc.alloc_sbuf_tensor_at(name, shape, dtype, offset=offset)

        def region(kilobytes):
            at[0] += kilobytes * KB
            return at[0] - kilobytes * KB

        raw = place("raw", [P, 2, KT * P])
        wh = place("wh", [P, 2, KT * P], F32R)
        wl = place("wl", [P, 2, KT * P], F32R)
        xh = place("xh", [P, KT, SEQ], F32R)
        xl = place("xl", [P, KT, SEQ], F32R)
        m_at = region(32)
        stream = place("stream", [P, KT, SEQ], offset=m_at)
        decay = place("decay", [P, 2, SEQ], offset=m_at)
        root0 = place("root0", [P, 2, SEQ], offset=m_at + 8 * KB)
        gated0 = place("gated0", [P, 2, SEQ], offset=m_at + 16 * KB)
        hsum = place("hsum", [P, 2, SEQ], offset=m_at + 24 * KB)
        y_at = region(64)
        yh = place("yh", [P, KT, SEQ], F32R, offset=y_at)
        yl = place("yl", [P, KT, SEQ], F32R, offset=y_at + 32 * KB)
        yah = place("yah", [P, ATT_KT, SEQ], F32R, offset=y_at)
        yal = place("yal", [P, ATT_KT, SEQ], F32R, offset=y_at + 16 * KB)
        scores = place("scores", [P, N_UNITS, HALF], offset=y_at + 32 * KB)
        values = place("values", [P, N_GROUPS, KT, P], offset=y_at + 32 * KB + N_UNITS * 2 * KB)
        mh = place("mh", [P, KT, SEQ], F32R, offset=y_at + 32 * KB)
        ml = place("ml", [P, KT, SEQ], F32R, offset=y_at)
        xf = place("xf", [P, 4, SEQ], offset=y_at + 16 * KB)
        xs = place("xs", [P, 2, SEQ], offset=y_at + 48 * KB)
        sq_pool = place("sq_pool", [P, 2, SEQ], offset=y_at + 48 * KB)
        lam_t = place("lam_t", [P, 6, 2 * KT], offset=y_at + 60 * KB)
        t_at = region(32)
        xc = place("xc", [P, 2, SEQ], offset=t_at)
        silu = place("silu", [P, 2, SEQ], offset=t_at + 8 * KB)
        root1 = place("root1", [P, 2, SEQ], offset=t_at + 16 * KB)
        gated1 = place("gated1", [P, 2, SEQ], offset=t_at + 24 * KB)
        gate = place("gate", [P, 2, SEQ], offset=t_at)
        qT = place("qT", [P, SEQ], offset=t_at)
        kT = place("kT", [P, SEQ], offset=t_at + 4 * KB)
        vT = place("vT", [P, SEQ], offset=t_at + 8 * KB)
        pT = place("pT", [P, 3, HALF], offset=t_at + 12 * KB)
        acc = place("acc", [P, SEQ], offset=t_at + 20 * KB)
        rden = place("rden", [P, SEQ], offset=t_at + 24 * KB)
        silu_a = place("silu_a", [P, SEQ], offset=t_at + 28 * KB)
        xold = place("xold", [P, 2, SEQ], offset=t_at + 8 * KB)
        sq = place("sq", [P, 2, SEQ], offset=t_at + 16 * KB)
        sumsq = place("sumsq", [P, SEQ], offset=t_at + 24 * KB)
        diag = place("diag", [P, KT, P], offset=t_at + 28 * KB)
        bias = place("bias", [P, N_BIAS])
        ident = place("ident", [P, P])
        ones = place("ones", [P, P])
        par_all = place("par_all", [P, DEPTH, N_PAR])
        par = place("par", [P, N_PAR])
        half = place("half", [P, N_HALF])
        decay_k = place("decay_k", [P, 2 * KT])
        half_k = place("half_k", [P, 2 * KT])
        norm_g = place("norm_g", [P, (DEPTH + 1) * KT])
        eps = place("eps", [P, 1])
        rms = place("rms", [P, KT])
        rinv = place("rinv", [P, KT])
        warm = place("warm", [P, 1])
        rowmax = place("rowmax", [P, N_STATS])
        negmax = place("negmax", [P, N_STATS])
        den = place("den", [P, N_STATS])
        stat_c = place("stat_c", [P, N_GROUPS, KT])
        stat_t = place("stat_t", [P, 3, KT])

        pair = [ctx.enter_context(nc.psum_tensor(f"pair{n}", [P, SEQ], F32)) for n in range(4)]
        bank = [pair[2][:, n * HALF:(n + 1) * HALF] for n in range(2)]

        kept = nc.dram_tensor("kept", [KT, P, SEQ], F32, kind="Internal").ap()
        max_d = nc.dram_tensor("max_d", [N_GROUPS, SEQ], F32, kind="Internal").ap()
        den_d = nc.dram_tensor("den_d", [N_GROUPS, SEQ], F32, kind="Internal").ap()
        negmax_d = nc.dram_tensor("negmax_d", [SEQ], F32, kind="Internal").ap()
        rden_d = nc.dram_tensor("rden_d", [1, SEQ], F32, kind="Internal").ap()

        def hold(engine, semaphore, value):
            if not isinstance(value, int):
                value = engine.to_reg(value)
            engine.wait_ge(started, 1)
            engine.wait_ge(semaphore, value)

        def one(i):
            return slice(i, i + 1) if isinstance(i, int) else bass.ds(i, 1)

        def col(table, i):
            return table[:, one(i)]

        def tile_of(tensor, i):
            return tensor[:, i, :] if isinstance(i, int) else tensor[:, bass.ds(i, 1), :].rearrange("p a s -> p (a s)")

        def stat_pieces(table, row, g):
            if g == 0:
                return [(table[:, 0:7], row[64:960].rearrange("(c p) -> p c", p=P)),
                        (table[0:64, 7:8], row[960:1024].rearrange("(p c) -> p c", c=1)),
                        (table[64:128, 7:8], row[0:64].rearrange("(p c) -> p c", c=1))]
            if g == 1:
                return [(table[:, 8:12], row[256:768].rearrange("(p r) -> p r", r=4)),
                        (table[0:64, 12:16], row[768:1024].rearrange("(p r) -> p r", r=4)),
                        (table[64:128, 12:16], row[0:256].rearrange("(p r) -> p r", r=4))]
            by_token = row.rearrange("(n b j) -> b n j", b=2, j=KT)
            return [(table[0:64, 16:24], by_token[0]), (table[64:128, 16:24], by_token[1])]

        def by_group(g, ap):
            if g == 0:
                return ap
            if g == 1:
                return ap.rearrange("p (n r) -> p r n", r=4)
            return ap.rearrange("p (n b j) -> p j b n", b=2, j=8)

        def in_group(g, ap):
            if g == 0:
                return ap
            if g == 1:
                return ap.rearrange("p (r n) -> p r n", r=4)
            return ap.rearrange("p (j b n) -> p j b n", b=2, j=8)

        block = ctx.enter_context(nc.Block())

        @block.sync
        def _(sp):
            def load(l, phase, i, k, width=KT * P):
                start = JOBS_START[phase]
                j = l * N_JOBS + i * JOBS[phase] + (start + k)
                hold(sp, w_lo.sem, w_lo.after(l, phase, i, k - 1))
                src = blocks[j] if isinstance(j, int) else blocks[bass.ds(j, 1)].rearrange("a p c -> (a p) c")
                sp.dma_start(raw[:, k % 2, 0:width], src[:, 0:width]).then_inc(raw_in[k % 2].sem, 16)

            def keep(n):
                kept_n = kept[n] if isinstance(n, int) else kept[bass.ds(n, 1)].rearrange("a p s -> (a p) s")
                sp.dma_start(kept_n, tile_of(stream, n)).then_inc(x_kept.sem, 16)

            def load_old(l, phase, i, first):
                for p in range(2):
                    hold(sp, pair_free[p].sem, pair_free[p].after(l, phase, i, 0))
                    n = KT - 2 + p if phase == "WOUTL" else i * 2 + p
                    src = kept[n] if isinstance(n, int) else kept[bass.ds(n, 1)].rearrange("a p s -> (a p) s")
                    sp.dma_start(xold[:, p, :], src).then_inc(xold_in[p].sem, 16)
                    if not first:
                        keep(n - 2)

            def send_max(l, phase, h, g):
                for use in range(SCORES_AT[g] + len(UNITS_OF[g]) - 2, SCORES_AT[g] + len(UNITS_OF[g])):
                    b = bank_free[use % 2]
                    hold(sp, b.sem, b.after(l, phase, h, use // 2 + 1))
                for sbuf, dram in stat_pieces(rowmax, max_d[g], g):
                    sp.dma_start(dram, sbuf, allow_slow_non_contiguous=True).then_inc(max_out.sem, 16)

            def exchange_max(l, phase, h, next_bias):
                send_max(l, phase, h, 2)
                sp.dma_start(bias[:], next_bias).then_inc(bias_in.sem, 16)
                hold(sp, max_out.sem, max_out.after(l, phase, h, 8))
                sp.dma_start(stat_c[:], max_d.rearrange("g (p i) -> p g i", i=KT)).then_inc(max_in.sem, 16)
                hold(sp, max_step.sem, max_step.after(l, phase, h, 3))
                sp.dma_start(negmax_d.rearrange("(p i) -> p i", i=KT), stat_t[:, 2, :]).then_inc(negmax_out.sem, 16)
                hold(sp, negmax_out.sem, negmax_out.after(l, phase, h, 1))
                for g in range(N_GROUPS):
                    for sbuf, dram in stat_pieces(negmax, negmax_d, g):
                        sp.dma_start(sbuf, dram, allow_slow_non_contiguous=True).then_inc(negmax_in[g].sem, 16)

            def exchange_den(l, phase, h):
                for g in range(N_GROUPS):
                    hold(sp, exp_done.sem, exp_done.after(l, phase, h, UNITS_OF[g].stop))
                    for sbuf, dram in stat_pieces(den, den_d[g], g):
                        sp.dma_start(dram, sbuf, allow_slow_non_contiguous=True).then_inc(den_out.sem, 16)
                hold(sp, den_out.sem, den_out.after(l, phase, h, 8))
                sp.dma_start(stat_c[:], den_d.rearrange("g (p i) -> p g i", i=KT)).then_inc(den_in.sem, 16)
                hold(sp, den_step.sem, den_step.after(l, phase, h, 3))
                sp.dma_start(rden_d[0].rearrange("(p i) -> p i", i=KT), stat_t[:, 2, :]).then_inc(rden_out.sem, 16)
                hold(sp, rden_out.sem, rden_out.after(l, phase, h, 1))
                hold(sp, asm_step.sem, asm_step.after(l, phase, h, 0))
                sp.dma_start(rden[:], rden_d.broadcast_to([P, SEQ])).then_inc(rden_in.sem, 16)

            def loads(l, phase, i, ks, width=KT * P):
                for k in ks:
                    load(l, phase, i, k, width)

            def slot_loads(l, phase, h):
                loads(l, phase, h, range(2, 4))
                send_max(l, phase, h, 0)
                loads(l, phase, h, range(4, 7))
                send_max(l, phase, h, 1)
                loads(l, phase, h, range(7, 10))

            sp.dma_start(norm_g[:], norm_table).then_inc(gain_in, 16)
            for n in range(KT):
                sp.dma_start(stream[:, n, :], xT[n]).then_inc(x_in[n], 16)
                if n in BLOCK_AFTER:
                    loads(0, "PRE", 0, [BLOCK_AFTER.index(n)])
            for table, source in ((ident, identity), (par_all, params)):
                sp.dma_start(table[:], source).then_inc(const_in, 16)
            sp.dma_start(bias[:], bias_table[0]).then_inc(bias_in.sem, 16)
            for n in range(KT):
                sp.wait_ge(x_in[n], 16)
                keep(n)
            with sp.Fori(0, DEPTH) as l:
                loads(l, "LRU", 0, range(2))
                with sp.Fori(0, 3) as b:
                    loads(l, "LRU", b, range(2, 6))
                    loads(l, "LRU", b + 1, range(2))
                loads(l, "LRUL", 0, range(2, 8))
                with sp.Fori(0, 2) as i:
                    loads(l, "LMIX", i, range(4))
                loads(l, "LMIXL", 0, range(4))
                loads(l, "QK", 0, range(2))
                loads(l, "ATT", 0, range(2))
                slot_loads(l, "ATT", 0)
                with sp.Fori(0, 2) as h:
                    loads(l, "ATT", h + 1, range(1))
                    exchange_max(l, "ATT", h, bias_table[bass.ds(h + 1, 1)].rearrange("a p c -> (a p) c"))
                    loads(l, "ATT", h + 1, range(1, 2))
                    exchange_den(l, "ATT", h)
                    slot_loads(l, "ATT", h + 1)
                loads(l, "ATTL", 0, range(1))
                exchange_max(l, "ATT", 2, bias_table[3])
                loads(l, "ATTL", 0, range(1, 2))
                exchange_den(l, "ATT", 2)
                slot_loads(l, "ATTL", 0)
                loads(l, "AMIX", 0, range(1), ATT_OUT)
                exchange_max(l, "ATTL", 0, bias_table[0])
                loads(l, "AMIX", 0, range(1, 2), ATT_OUT)
                exchange_den(l, "ATTL", 0)
                loads(l, "AMIX", 0, range(2, 4))
                with sp.Fori(1, 3) as i:
                    loads(l, "AMIX", i, range(2), ATT_OUT)
                    loads(l, "AMIX", i, range(2, 4))
                loads(l, "AMIXL", 0, range(2), ATT_OUT)
                loads(l, "WOUT", 0, range(2))
                load_old(l, "WOUT", 0, True)
                with sp.Fori(1, 3) as i:
                    loads(l, "WOUT", i, range(2))
                    load_old(l, "WOUT", i, False)
                loads(l, "WOUTL", 0, range(2))
                load_old(l, "WOUTL", 0, False)
                loads(l + 1, "PRE", 0, range(2))
                for p in range(2):
                    hold(sp, pair_free[p].sem, pair_free[p].after(l, "WOUTL", 0, 1))
                    keep(KT - 2 + p)
            for n in range(KT):
                sp.wait_ge(fin_ready, n + 1)
                sp.dma_start(outT[n], stream[:, n, :]).then_inc(out_done, 16)
            sp.wait_ge(x_kept.sem, x_kept.after(DEPTH, "PRE", 0, 0))
            sp.wait_ge(out_done, 16 * KT)

        @block.scalar
        def _(act):
            def split_hi(l, phase, i, k, width=KT * P):
                r = raw_in[k % 2]
                act.wait_ge(r.sem, r.after(l, phase, i, k // 2 + 1))
                act.activation(wh[:, k % 2, 0:width], raw[:, k % 2, 0:width], ACT.Copy).then_inc(w_hi.sem, 1)

            def job(l, phase, i, k):
                act.wait_ge(job_done.sem, job_done.after(l, phase, i, k))

            def warm_up(l):
                act.wait_ge(warmed.sem, warmed.after(l, "PRE", 0, 0))
                act.activation(warm[:], warm[:], ACT.Sqrt).then_inc(warmed.sem, 1)

            def root_mean_square(l):
                act.wait_ge(norm_done.sem, norm_done.after(l, "PRE", 0, 1))
                act.activation(rms[:], pair[2][:, 0:KT], ACT.Sqrt, bias=eps[:], scale=1.0 / D_MODEL)\
                    .then_inc(pair_free[2].sem, 1)

            def take_x(l, t):
                job(l, "PRE", 0, t + 1)
                act.activation(xs[:, t, :], pair[t][:], ACT.Copy).then_inc(pair_free[t].sem, 1)

            def xn_hi(l, k):
                if k < KT - 1:
                    act.wait_ge(x_used.sem, x_used.after(l, "PRE", 0, k + 1))
                else:
                    job(l, "PRE", 0, 2)
                act.wait_ge(xf_ready.sem, xf_ready.after(l, "PRE", 0, k + 1))
                act.activation(xh[:, k, :], xf[:, k % 4, :], ACT.Copy).then_inc(xh_ready.sem, 1)

            def start_conv(l, phase, i, b, t):
                c = b * TPB + t
                x = xs[:, t, :] if phase == "PRE" else pair[t][:]
                act.activation(xc[:, t, :], x, ACT.Identity, scale=col(par, c + (PAR_CONV + 2 * KT)),
                               bias=col(par, c + PAR_CONV_B)).then_inc(conv_init.sem, 1)

            def split_xc(l, phase, i, b, t, frees):
                if phase == "PRE":
                    act.wait_ge(conv_step.sem, conv_step.after(l, phase, i, 3 * t + 3))
                else:
                    act.wait_ge(pair_free[t].sem, pair_free[t].after(l, phase, i, frees))
                act.activation(tile_of(yh, b * TPB + t), xc[:, t, :], ACT.Copy).then_inc(xc_hi.sem, 1)

            def square(tile, p):
                act.activation(sq[:, p, :], tile, ACT.Square).then_inc(sq_ready.sem, 1)

            def rec_tanh(l, phase, i, b, o):
                d, t, which = o // 4, o // 2 % 2, o % 2
                q = (2 + o) % 4
                to = ((root0, gated0), (root1, gated1))[d][which]
                act.wait_ge(rg_done.sem, rg_done.after(l, phase, i, o + 1))
                bias_at = b * TPB + ((HALF_RGA, HALF_RGX)[which] + d * KT + t)
                act.activation(to[:, t, :], pair[q][:], ACT.Tanh, scale=0.5, bias=col(half, bias_at))\
                    .then_inc(pair_free[q].sem, 1)

            def rec_decay(l, phase, i, b, d):
                root = (root0, root1)[d]
                for t in range(2):
                    q = (2 + d * 4 + t * 2) % 4
                    act.wait_ge(pair_free[q].sem, pair_free[q].after(l, phase, i, RG_FREES[d * 4 + t * 2]))
                    if d == 1:
                        act.wait_ge(rec_step.sem, rec_step.after(l, phase, i, 9 + t))
                    k = b * TPB + (d * KT + t)
                    act.activation(decay[:, t, :], root[:, t, :], ACT.Exp, scale=col(decay_k, k), bias=col(decay_k, k))\
                        .then_inc(decay_ready.sem, 1)
                for t in range(2):
                    k = b * TPB + (d * KT + t)
                    act.activation(root[:, t, :], root[:, t, :], ACT.Tanh, scale=col(half_k, k), bias=col(half_k, k))\
                        .then_inc(half_decay.sem, 1)

            def rec_root(l, phase, i, d):
                root = (root0, root1)[d]
                act.wait_ge(half_decay.sem, half_decay.after(l, phase, i, 2 * d + 2))
                for t in range(2):
                    act.activation(root[:, t, :], root[:, t, :], ACT.Sqrt).then_inc(root_ready.sem, 1)

            def silu_start(l, phase, i, t):
                job(l, phase, i, t + 1)
                act.activation(silu[:, t, :], pair[t][:], ACT.Tanh, scale=0.5).then_inc(silu_tanh.sem, 1)

            def merge_gate(l, branch, m, p):
                act.activation(tile_of(stream, m) if branch else gate[:, p, :], pair[p][:], ACT.Tanh, scale=0.5,
                               bias=col(half, m + (HALF_GATT, HALF_GLRU)[branch])).then_inc(pair_free[p].sem, 1)

            def lru(l, phase, i, b, last):
                for t in range(2):
                    silu_start(l, phase, i, t)
                split_hi(l, phase, i, 3)
                for o in range(4):
                    rec_tanh(l, phase, i, b, o)
                split_hi(l, phase, i, 4)
                rec_decay(l, phase, i, b, 0)
                for o in range(4, 8):
                    rec_tanh(l, phase, i, b, o)
                split_hi(l, phase, i, 5)
                rec_root(l, phase, i, 0)
                act.wait_ge(rec_step.sem, rec_step.after(l, phase, i, 4))
                job(l, phase, i, 3)
                if last:
                    split_hi(l, phase, i, 6)
                else:
                    start_conv(l, phase, i, b + 1, 0)
                    split_next(l, phase, i, 0)
                rec_decay(l, phase, i, b, 1)
                if last:
                    merge_gate(l, 1, 2, 0)
                else:
                    split_xc(l, phase, i, b + 1, 0, PAIR_LRU[0])
                rec_root(l, phase, i, 1)
                job(l, phase, i, 4)
                if last:
                    merge_gate(l, 1, 3, 1)
                    split_hi(l, phase, i, 7)
                    job(l, phase, i, 5)
                    merge_gate(l, 1, 4, 0)
                    split_hi(l, "LMIX", 0, 0)
                else:
                    start_conv(l, phase, i, b + 1, 1)
                    split_next(l, phase, i, 1)
                    split_xc(l, phase, i, b + 1, 1, PAIR_LRU[1])
                    job(l, phase, i + 1, 1)
                    split_next(l, phase, i, 2)
                for t in range(2):
                    act.wait_ge(rec_step.sem, rec_step.after(l, phase, i, 18 + 2 * t))
                    act.activation(tile_of(yh, b * TPB + t), hsum[:, t, :], ACT.Copy).then_inc(y_hi.sem, 1)
                if last:
                    job(l, phase, i, 6)
                    merge_gate(l, 1, 5, 1)
                    split_hi(l, "LMIX", 0, 1)

            def split_next(l, phase, i, k):
                r = raw_in[k % 2]
                act.wait_ge(r.sem, r.after(l, phase, i + 1, k // 2 + 1))
                act.activation(wh[:, k % 2, :], raw[:, k % 2, :], ACT.Copy).then_inc(w_hi.sem, 1)

            def mix(l, phase, i, branch):
                width = KT * P
                for p in range(2):
                    job(l, phase, i, p + 1)
                    split_hi(l, phase, i, p + 2)
                for p in range(2):
                    job(l, phase, i, p + 3)
                    if not branch:
                        act.wait_ge(mix_done.sem, mix_done.after(l, phase, i, p + 1))
                    merge_gate(l, branch, i * 6 + p if branch else i * 2 + (2 + p), p)
                    r = raw_in[p]
                    act.wait_ge(r.sem, r.after(l, phase, i + 1, 1))
                    act.activation(wh[:, p, 0:(ATT_OUT, width)[branch]], raw[:, p, 0:(ATT_OUT, width)[branch]],
                                   ACT.Copy).then_inc(w_hi.sem, 1)

            def qkv(l, phase, i, k, which, g, to, p):
                job(l, phase, i, k + 1)
                act.activation(in_group(g, to[:]), by_group(g, pair[p][:]), ACT.Copy,
                               scale=SCALE if which == "q" else 1.0).then_inc(pair_free[p].sem, 1)

            def take_values(l, phase, h, g):
                for n in range(2):
                    use = VT_AT[g] + n
                    act.wait_ge(unit_ready.sem, unit_ready.after(l, phase, h, use + 1))
                    act.activation(values[:, g, 4 * n:4 * n + 4, :].rearrange("p c d -> p (c d)"), bank[use % 2],
                                   ACT.Copy).then_inc(bank_free[use % 2].sem, 1)

            def exps(l, phase, h):
                for u, tiles in enumerate(UNITS):
                    group = tiles[0][0]
                    if u == UNITS_OF[group].start:
                        n = negmax_in[group]
                        act.wait_ge(n.sem, n.after(l, phase, h, (3, 3, 2)[group]))
                    for n, (g, kind, idx, column, width, stat) in enumerate(tiles):
                        s = scores[:, u, column:column + width]
                        e = act.activation(s, s, ACT.Exp, bias=negmax[:, stat:stat + 1],
                                           accum_out=den[:, stat:stat + 1])
                    e.then_inc(exp_done.sem, 1)

            def assemble(l, phase, h):
                act.wait_ge(pv_done.sem, pv_done.after(l, phase, h, 1))
                act.activation(acc[:, 64:SEQ], pair[3][:, 0:SEQ - 64], ACT.Copy).then_inc(asm_start.sem, 1)
                act.activation(acc[:, 0:64], pair[3][:, SEQ - 64:SEQ], ACT.Copy).then_inc(pair_free[3].sem, 1)
                act.wait_ge(asm_step.sem, asm_step.after(l, phase, h, 3))
                slot = HEADS_PER_GROUP - 1 if phase == "ATTL" else h
                act.activation(tile_of(yah, slot), acc[:], ACT.Copy, scale=0.5).then_inc(ya_hi.sem, 1)

            def attention(l, phase, h, last):
                dst = {"q": qT, "k": kT, "v": vT}
                order = [("v", 0), ("q", 1), ("k", 1), ("v", 1), ("q", 2), ("k", 2), ("v", 2)]
                for k, (which, g) in enumerate(order):
                    qkv(l, phase, h, k, which, g, dst[which], k % 2)
                    split_hi(l, phase, h, k + 2)
                    if (which, g) == ("q", 1):
                        take_values(l, phase, h, 0)
                    if (which, g) == ("q", 2):
                        take_values(l, phase, h, 1)
                job(l, phase, h, 8)
                act.activation(silu_a[:], pair[1][:], ACT.Tanh, scale=0.5).then_inc(silu_tanh.sem, 1)
                split_hi(l, phase, h, 9)
                take_values(l, phase, h, 2)
                exps(l, phase, h)
                if last:
                    job(l, phase, h, 9)
                    merge_gate(l, 0, 0, 0)
                    split_hi(l, "AMIX", 0, 0, ATT_OUT)
                    assemble(l, phase, h)
                    job(l, phase, h, 10)
                    merge_gate(l, 0, 1, 1)
                    split_hi(l, "AMIX", 0, 1, ATT_OUT)
                else:
                    qkv(l, phase, h, 8, "q", 0, qT, 0)
                    split_next(l, phase, h, 0)
                    qkv(l, phase, h, 9, "k", 0, kT, 1)
                    split_next(l, phase, h, 1)
                    assemble(l, phase, h)

            def split_merged(l, m):
                act.wait_ge(mix_done.sem, mix_done.after(l, "AMIX", 0, m + 1))
                act.activation(mh[:, m, :], stream[:, m, :], ACT.Copy).then_inc(mh_ready.sem, 1)

            def gain_hi(tile, n, gain):
                act.activation(tile_of(xh, n), tile, ACT.Copy, scale=col(norm_g, gain)).then_inc(xg_hi.sem, 1)

            def take_new(l, phase, i, p, n):
                act.wait_ge(sumsq_step.sem, sumsq_step.after(l, phase, i, p - 1))
                act.wait_ge(pair_free[p].sem, pair_free[p].after(l, phase, i, 1))
                if phase == "WOUTL":
                    square(tile_of(stream, n), p)
                gain_hi(tile_of(stream, n), n, l * KT + (KT + n))
                if phase == "WOUT":
                    square(tile_of(stream, n), p)

            act.wait_ge(gain_in, 16)
            for n in range(KT):
                act.wait_ge(x_in[n], 16)
                gain_hi(stream[:, n, :], n, n)
                if n in SQUARE_ACT:
                    m = SQUARE_ACT.index(n)
                    if m >= 2:
                        act.wait_ge(sumsq_step.sem, SQUARE_ACT[m - 2] + 2)
                    square(stream[:, n, :], m % 2)
                if n in BLOCK_AFTER:
                    split_hi(0, "PRE", 0, BLOCK_AFTER.index(n))

            with act.Fori(0, DEPTH) as l:
                act.wait_ge(par_step.sem, par_step.after(l, "PRE", 0, 3))
                act.activation(lam_t[:, 1, :], lam_t[:, 0, :], ACT.Exp, scale=-1.0).then_inc(lam_exp.sem, 1)
                warm_up(l)
                take_x(l, 0)
                root_mean_square(l)
                split_hi(l, "LRU", 0, 0)
                act.wait_ge(par_step.sem, par_step.after(l, "PRE", 0, 20))
                for k in range(KT):
                    xn_hi(l, k)
                    if k == SCALE_AT:
                        act.wait_ge(x_scaled.sem, x_scaled.after(l, "PRE", 0, 1))
                        start_conv(l, "PRE", 0, 0, 0)
                    if k == 3:
                        take_x(l, 1)
                        split_hi(l, "LRU", 0, 1)
                act.wait_ge(pair_free[3].sem, pair_free[3].after(l, "PRE", 0, 1))
                start_conv(l, "PRE", 0, 0, 1)
                for t in range(2):
                    split_xc(l, "PRE", 0, 0, t, 0)
                job(l, "LRU", 0, 1)
                split_hi(l, "LRU", 0, 2)
                act.wait_ge(x_kept.sem, x_kept.after(l, "PRE", 0, 0))
                with act.Fori(0, 3) as b:
                    lru(l, "LRU", b, b, False)
                lru(l, "LRUL", 0, 3, True)
                with act.Fori(0, 2) as i:
                    mix(l, "LMIX", i, 1)
                for k in range(4):
                    job(l, "LMIXL", 0, k + 1)
                    split_hi(l, ("LMIXL", "QK")[k // 2], 0, (k + 2) % 4)
                for p, (which, to) in enumerate((("q", qT), ("k", kT))):
                    qkv(l, "QK", 0, p, which, 0, to, p)
                    split_hi(l, "ATT", 0, p)
                with act.Fori(0, 3) as h:
                    attention(l, "ATT", h, False)
                attention(l, "ATTL", 0, True)
                with act.Fori(0, 3) as i:
                    mix(l, "AMIX", i, 0)
                for p in range(2):
                    for m in range(3 * p, 3 * p + 3):
                        split_merged(l, m)
                    job(l, "AMIXL", 0, p + 1)
                    split_hi(l, "WOUT", 0, p)
                split_merged(l, 6)
                split_merged(l, 7)
                with act.Fori(0, 3) as i:
                    for p in range(2):
                        job(l, "WOUT", i, p + 1)
                        split_next(l, "WOUT", i, p)
                        take_new(l, "WOUT", i, p, i * 2 + p)
                for p in range(2):
                    job(l, "WOUTL", 0, p + 1)
                    split_hi(l + 1, "PRE", 0, p)
                    take_new(l, "WOUTL", 0, p, KT - 2 + p)
            warm_up(DEPTH)
            root_mean_square(DEPTH)

        @block.gpsimd
        def _(pool):
            pool.memset(eps[:], EPS).then_inc(w_lo.sem, 1)
            pool.memset(ones[:], 1.0).then_inc(w_lo.sem, 1)
            pool.memset(negmax[:], 0.0).then_inc(started, 1)
            pool.memset(warm[:], 1.0).then_inc(warmed.sem, 1)

            def low(to, full, high, signal):
                pool.tensor_tensor(to, full, high.bitcast(F32), ALU.subtract).then_inc(signal.sem, 1)

            def split_lo(l, phase, i, k, width=KT * P):
                pool.wait_ge(w_hi.sem, w_hi.after(l, phase, i, k + 1))
                low(wl[:, k % 2, 0:width], raw[:, k % 2, 0:width], wh[:, k % 2, 0:width], w_lo)

            def split_next(l, phase, i, k, width=KT * P):
                pool.wait_ge(w_hi.sem, w_hi.after(l, phase, i + 1, k + 1))
                low(wl[:, k % 2, 0:width], raw[:, k % 2, 0:width], wh[:, k % 2, 0:width], w_lo)

            def low_xc(l, phase, i, b, t):
                pool.wait_ge(xc_hi.sem, xc_hi.after(l, phase, i, t + 1))
                low(tile_of(yl, b * TPB + t), xc[:, t, :], tile_of(yh, b * TPB + t), xc_lo)

            def low_y(l, phase, i, b, t):
                pool.wait_ge(y_hi.sem, y_hi.after(l, phase, i, t + 1))
                low(tile_of(yl, b * TPB + t), hsum[:, t, :], tile_of(yh, b * TPB + t), y_lo)

            def lru(l, phase, i, b, last):
                for k in range(3, 6):
                    split_lo(l, phase, i, k)
                if last:
                    for k in (6, 7):
                        split_lo(l, phase, i, k)
                    split_lo(l, "LMIX", 0, 0)
                else:
                    for t in range(2):
                        split_next(l, phase, i, t)
                        low_xc(l, phase, i, b + 1, t)
                    split_next(l, phase, i, 2)
                for t in range(2):
                    low_y(l, phase, i, b, t)
                if last:
                    split_lo(l, "LMIX", 0, 1)

            def clear_sum():
                pool.memset(sumsq[:], 0.0).then_inc(sumsq_step.sem, 1)

            def add_square(p, have, prior):
                pool.wait_ge(sq_ready.sem, have)
                pool.wait_ge(sumsq_step.sem, prior)
                pool.tensor_tensor(sumsq[:], sumsq[:], sq[:, p, :], ALU.add).then_inc(sumsq_step.sem, 1)

            clear_sum()
            for k in range(2):
                split_lo(0, "PRE", 0, k)
                pool.wait_ge(x_in[SQUARE_POOL[k]], 16)
                tile = stream[:, SQUARE_POOL[k], :]
                pool.tensor_tensor(sq_pool[:, k, :], tile, tile, ALU.mult).then_inc(sq_pool_ready, 1)

            with pool.Fori(0, DEPTH) as l:
                split_lo(l, "LRU", 0, 0)
                for k in range(1, KT, 2):
                    pool.wait_ge(xh_ready.sem, xh_ready.after(l, "PRE", 0, k + 1))
                    low(xl[:, k, :], xf[:, k % 4, :], xh[:, k, :], xl_pool)
                    if k == 3:
                        split_lo(l, "LRU", 0, 1)
                split_lo(l, "LRU", 0, 2)
                with pool.Fori(0, 3) as b:
                    lru(l, "LRU", b, b, False)
                lru(l, "LRUL", 0, 3, True)
                with pool.Fori(0, 2) as i:
                    for k in (2, 3):
                        split_lo(l, "LMIX", i, k)
                    for k in (0, 1):
                        split_next(l, "LMIX", i, k)
                for k in (2, 3):
                    split_lo(l, "LMIXL", 0, k)
                for phase in ("QK", "ATT"):
                    for k in (0, 1):
                        split_lo(l, phase, 0, k)
                with pool.Fori(0, 3) as h:
                    for k in range(2, 10):
                        split_lo(l, "ATT", h, k)
                    for k in (0, 1):
                        split_next(l, "ATT", h, k)
                for k in range(2, 10):
                    split_lo(l, "ATTL", 0, k)
                for k in (0, 1):
                    split_lo(l, "AMIX", 0, k, ATT_OUT)
                with pool.Fori(0, 3) as i:
                    for k in (2, 3):
                        split_lo(l, "AMIX", i, k)
                    for k in (0, 1):
                        split_next(l, "AMIX", i, k, ATT_OUT)
                split_lo(l, "WOUT", 0, 0)
                hold(pool, job_done.sem, job_done.after(l, "AMIXL", 0, 2))
                for n, m in enumerate(ML_POOL):
                    pool.wait_ge(mh_ready.sem, mh_ready.after(l, "AMIXL", 0, m + 1))
                    low(ml[:, m, :], stream[:, m, :], mh[:, m, :], ml_pool)
                    if n == 0:
                        split_lo(l, "WOUT", 0, 1)
                clear_sum()
                with pool.Fori(0, 3) as i:
                    for p in range(2):
                        split_next(l, "WOUT", i, p)
                        add_square(p, sq_ready.after(l, "WOUT", i, p + 1), sumsq_step.after(l, "WOUT", i, p))
                add_square(0, sq_ready.after(l, "WOUTL", 0, 1), sumsq_step.after(l, "WOUTL", 0, 0))
                for p in range(2):
                    split_lo(l + 1, "PRE", 0, p)

        @block.vector
        def _(dve):
            for n, s in enumerate([pair_free[0], pair_free[1], pair_free[2], pair_free[3], bank_free[0], bank_free[1],
                                   y_lo, asm_step]):
                dve.memset(rowmax[:, n:n + 1], 0.0).then_inc(s.sem, 1)
            dve.wait_ge(gain_in, 16)

            def gain_lo(tile, n, gain):
                dve.scalar_tensor_tensor(out=tile_of(xl, n), in0=tile, scalar=col(norm_g, gain),
                                         in1=tile_of(xh, n).bitcast(F32), op0=ALU.mult, op1=ALU.subtract)\
                    .then_inc(xg_lo.sem, 1)

            def normalise(l, final=False):
                dve.wait_ge(pair_free[2].sem, pair_free[2].after(l, "PRE", 0, 1))
                dve.reciprocal(rinv[:], rms[:]).then_inc(norm_step.sem, 1)
                dve.wait_ge(norm_step.sem, norm_step.after(l, "PRE", 0, 1))
                dve.tensor_tensor(diag[:], ident[:].unsqueeze(1).broadcast_to([P, KT, P]),
                                  rinv[:].unsqueeze(2).broadcast_to([P, KT, P]), ALU.mult).then_inc(norm_step.sem, 1)
                dve.wait_ge(norm_done.sem, norm_done.after(l, "PRE", 0, 2))
                if final:
                    dve.wait_ge(x_kept.sem, x_kept.after(l, "PRE", 0, 0))
                    for k in range(KT):
                        dve.scalar_tensor_tensor(out=stream[:, k, :], in0=stream[:, k, :],
                                                 scalar=col(norm_g, DEPTH * KT + k), in1=pair[3][:],
                                                 op0=ALU.mult, op1=ALU.mult).then_inc(fin_ready, 1)
                    return
                for k in range(KT):
                    if k >= 4 and k % 2:
                        dve.wait_ge(xl_pool.sem, xl_pool.after(l, "PRE", 0, k // 2 - 1))
                    elif k >= 4:
                        dve.wait_ge(xl_dve.sem, xl_dve.after(l, "PRE", 0, k // 2 - 1))
                    dve.scalar_tensor_tensor(out=xf[:, k % 4, :], in0=stream[:, k, :], scalar=col(norm_g, l * KT + k),
                                             in1=pair[3][:], op0=ALU.mult, op1=ALU.mult).then_inc(xf_ready.sem, 1)
                    if k % 2:
                        dve.wait_ge(xh_ready.sem, xh_ready.after(l, "PRE", 0, k))
                        dve.tensor_tensor(xl[:, k - 1, :], xf[:, (k - 1) % 4, :], xh[:, k - 1, :].bitcast(F32),
                                          ALU.subtract).then_inc(xl_dve.sem, 1)
                    if k == SCALE_AT:
                        dve.wait_ge(pair_free[0].sem, pair_free[0].after(l, "PRE", 0, 1))
                        dve.tensor_tensor(xs[:, 0, :], xs[:, 0, :], pair[3][:], ALU.mult).then_inc(x_scaled.sem, 1)
                dve.wait_ge(pair_free[1].sem, pair_free[1].after(l, "PRE", 0, 1))
                dve.tensor_tensor(xs[:, 1, :], xs[:, 1, :], pair[3][:], ALU.mult).then_inc(pair_free[3].sem, 1)

            def prepare(l):
                n = [1]

                def step(instruction):
                    instruction.then_inc(par_step.sem, 1)
                    n[0] += 1
                    dve.wait_ge(par_step.sem, par_step.after(l, "PRE", 0, n[0]))

                dve.wait_ge(par_step.sem, par_step.after(l, "PRE", 0, 1))
                lam = par[:, PAR_LAM:PAR_LAM + 2 * KT]
                step(dve.tensor_scalar(half[:], par[:, PAR_GATE:PAR_GATE + N_HALF], 0.5, None, ALU.mult))
                step(dve.scalar_tensor_tensor(out=lam_t[:, 0, :], in0=lam, scalar=-1.0, in1=lam, op0=ALU.mult,
                                              op1=ALU.max))
                step(dve.tensor_scalar(lam_t[:, 5, :], lam, -1.0, 0.0, ALU.mult, ALU.max))
                dve.wait_ge(lam_exp.sem, lam_exp.after(l, "PRE", 0, 1))
                step(dve.tensor_scalar(lam_t[:, 2, :], lam_t[:, 1, :], 2.0, None, ALU.add))
                step(dve.reciprocal(lam_t[:, 3, :], lam_t[:, 2, :]))
                step(dve.tensor_tensor(lam_t[:, 2, :], lam_t[:, 3, :], lam_t[:, 1, :], ALU.mult))
                step(dve.tensor_tensor(lam_t[:, 3, :], lam_t[:, 2, :], lam_t[:, 2, :], ALU.mult))
                step(dve.tensor_scalar(lam_t[:, 4, :], lam_t[:, 3, :], 1.0 / 17, None, ALU.mult))
                for odd in range(15, 1, -2):
                    step(dve.scalar_tensor_tensor(out=lam_t[:, 4, :], in0=lam_t[:, 4, :], scalar=1.0 / odd,
                                                  in1=lam_t[:, 3, :], op0=ALU.add, op1=ALU.mult))
                step(dve.scalar_tensor_tensor(out=lam_t[:, 4, :], in0=lam_t[:, 4, :], scalar=1.0, in1=lam_t[:, 2, :],
                                              op0=ALU.add, op1=ALU.mult))
                step(dve.scalar_tensor_tensor(out=lam_t[:, 3, :], in0=lam_t[:, 4, :], scalar=2.0, in1=lam_t[:, 5, :],
                                              op0=ALU.mult, op1=ALU.add))
                step(dve.tensor_scalar(decay_k[:], lam_t[:, 3, :], -4.0, None, ALU.mult))
                step(dve.tensor_scalar(half_k[:], lam_t[:, 3, :], 2.0, None, ALU.mult))
                assert n[0] == 20

            def conv(l, phase, i, b, t):
                c = b * TPB + t
                dve.wait_ge(conv_init.sem, conv_init.after(l, phase, i, t + 1))
                taken = phase == "PRE"
                x = xs[:, t, :] if taken else pair[t][:]
                for n, tap in enumerate((0, 1, 3)):
                    shift = tap - 2
                    lo, hi = max(0, -shift), SEQ - max(0, shift)
                    if n:
                        dve.wait_ge(conv_step.sem, conv_step.after(l, phase, i, (3 if taken else 2) * t + n))
                    dve.scalar_tensor_tensor(out=xc[:, t, lo:hi], in0=x[:, lo + shift:hi + shift],
                                             scalar=col(par, c + (PAR_CONV + tap * KT)), in1=xc[:, t, lo:hi],
                                             op0=ALU.mult, op1=ALU.add)\
                        .then_inc((conv_step, conv_step, conv_step if taken else pair_free[t])[n].sem, 1)

            def lru(l, phase, i, b, last):
                def after(k):
                    dve.wait_ge(rec_step.sem, rec_step.after(l, phase, i, k))

                for t in range(2):
                    dve.wait_ge(silu_tanh.sem, silu_tanh.after(l, phase, i, t + 1))
                    dve.scalar_tensor_tensor(out=silu[:, t, :], in0=silu[:, t, :], scalar=1.0, in1=pair[t][:],
                                             op0=ALU.add, op1=ALU.mult).then_inc(pair_free[t].sem, 1)
                for d in range(2):
                    for t in range(2):
                        o = d * 4 + t * 2 + 1
                        q = (2 + o) % 4
                        dve.wait_ge(pair_free[q].sem, pair_free[q].after(l, phase, i, RG_FREES[o]))
                        gated = (gated0, gated1)[d]
                        dve.scalar_tensor_tensor(out=gated[:, t, :], in0=gated[:, t, :], scalar=1.0, in1=xc[:, t, :],
                                                 op0=ALU.add, op1=ALU.mult).then_inc(rec_step.sem, 1)
                for d in range(2):
                    gated, root = (gated0, gated1)[d], (root0, root1)[d]
                    s = 5 + 6 * d
                    inner = slice(1, SEQ) if d == 0 else slice(0, SEQ - 1)
                    for t in range(2):
                        dve.wait_ge(decay_ready.sem, decay_ready.after(l, phase, i, 2 * d + t + 1))
                        after(1 + 2 * d + t)
                        dve.scalar_tensor_tensor(out=gated[:, t, inner], in0=decay[:, t, inner], scalar=1.0,
                                                 in1=gated[:, t, inner], op0=ALU.add, op1=ALU.mult)\
                            .then_inc(rec_step.sem, 1)
                    for t in range(2):
                        dve.wait_ge(root_ready.sem, root_ready.after(l, phase, i, 2 * d + t + 1))
                        after(s + t)
                        dve.tensor_tensor(gated[:, t, inner], gated[:, t, inner], root[:, t, inner], ALU.mult)\
                            .then_inc(rec_step.sem, 1)
                    for t in range(2):
                        after(s + 2 + t)
                        if d == 0:
                            if t == 0:
                                dve.wait_ge(y_lo.sem, y_lo.after(l, phase, i, 0))
                            dve.tensor_tensor_scan(hsum[:, t, :], decay[:, t, :], gated[:, t, :], 0.0, op0=ALU.mult,
                                                   op1=ALU.add).then_inc(rec_step.sem, 1)
                        else:
                            dve.tensor_tensor_scan(root[:, t, ::-1], decay[:, t, ::-1], gated[:, t, ::-1], 0.0,
                                                   op0=ALU.mult, op1=ALU.add).then_inc(rec_step.sem, 1)
                    if not last:
                        conv(l, phase, i, b + 1, d)
                for t in range(2):
                    after(15 + t)
                    dve.tensor_tensor(hsum[:, t, :], hsum[:, t, :], root1[:, t, :], ALU.add).then_inc(rec_step.sem, 1)
                    after(17 + 2 * t)
                    dve.scalar_tensor_tensor(out=hsum[:, t, :], in0=hsum[:, t, :], scalar=0.25, in1=silu[:, t, :],
                                             op0=ALU.mult, op1=ALU.mult).then_inc(rec_step.sem, 1)

            def mix_lru(l, phase, i, k, m):
                p = k % 2
                dve.wait_ge(job_done.sem, job_done.after(l, phase, i, k + 1))
                dve.wait_ge(pair_free[p].sem, pair_free[p].after(l, phase, i, k // 2))
                dve.scalar_tensor_tensor(out=tile_of(stream, m), in0=tile_of(stream, m), scalar=1.0, in1=pair[p][:],
                                         op0=ALU.add, op1=ALU.mult).then_inc(pair_free[p].sem, 1)

            def mix_att(l, phase, i, p, m):
                dve.wait_ge(job_done.sem, job_done.after(l, phase, i, p + 1))
                dve.wait_ge(pair_free[p].sem, pair_free[p].after(l, phase, i, 0))
                dve.scalar_tensor_tensor(out=gate[:, p, :], in0=gate[:, p, :], scalar=1.0, in1=pair[p][:],
                                         op0=ALU.add, op1=ALU.mult).then_inc(pair_free[p].sem, 1)
                dve.wait_ge(pair_free[p].sem, pair_free[p].after(l, phase, i, 1))
                dve.tensor_tensor(tile_of(stream, m), tile_of(stream, m), gate[:, p, :], ALU.add)\
                    .then_inc(mix_done.sem, 1)

            def score_rows(l, phase, h, g):
                for n, u in enumerate(UNITS_OF[g]):
                    use = SCORES_AT[g] + n
                    hold(dve, unit_ready.sem, unit_ready.after(l, phase, h, use + 1))
                    for _, kind, idx, column, width, stat in UNITS[u]:
                        at_bias = BIAS_AT[g, kind]
                        e = dve.tensor_tensor_reduce(
                            scores[:, u, column:column + width], bank[use % 2][:, column:column + width],
                            bias[:, at_bias:at_bias + width], 1.0, -3e38, ALU.add, ALU.max, rowmax[:, stat:stat + 1])
                    e.then_inc(bank_free[use % 2].sem, 1)

            def combine(arrived, steps, l, phase, h, op):
                dve.wait_ge(arrived.sem, arrived.after(l, phase, h, 1))
                dve.tensor_tensor(stat_t[:, 0, :], stat_c[:, 0, :], stat_c[:, 1, :], op).then_inc(steps.sem, 1)
                dve.wait_ge(steps.sem, steps.after(l, phase, h, 1))
                dve.tensor_tensor(stat_t[:, 1, :], stat_t[:, 0, :], stat_c[:, 2, :], op).then_inc(steps.sem, 1)
                dve.wait_ge(steps.sem, steps.after(l, phase, h, 2))
                if op == ALU.max:
                    dve.tensor_scalar(stat_t[:, 2, :], stat_t[:, 1, :], -1.0, None, ALU.mult).then_inc(steps.sem, 1)
                else:
                    dve.reciprocal(stat_t[:, 2, :], stat_t[:, 1, :]).then_inc(steps.sem, 1)

            def attention(l, phase, h, last):
                dve.wait_ge(bias_in.sem, bias_in.after(l, phase, h, 0))
                for g in range(N_GROUPS):
                    score_rows(l, phase, h, g)
                combine(max_in, max_step, l, phase, h, ALU.max)
                dve.wait_ge(silu_tanh.sem, silu_tanh.after(l, phase, h, 1))
                dve.scalar_tensor_tensor(out=silu_a[:], in0=silu_a[:], scalar=1.0, in1=pair[1][:], op0=ALU.add,
                                         op1=ALU.mult).then_inc(pair_free[1].sem, 1)
                for u in range(N_UNITS):
                    use = PT_AT + u
                    width = sum(t[4] for t in UNITS[u])
                    dve.wait_ge(unit_ready.sem, unit_ready.after(l, phase, h, use + 1))
                    dve.tensor_copy(pT[:, u % 3, 0:width], bank[use % 2][:, 0:width]).then_inc(bank_free[use % 2].sem, 1)
                    if u == 6 and not last:
                        combine(den_in, den_step, l, phase, h, ALU.add)
                dve.wait_ge(pair_free[3].sem, pair_free[3].after(l, phase, h, 1))
                dve.wait_ge(asm_start.sem, asm_start.after(l, phase, h, 1))
                dve.wait_ge(pv_done.sem, pv_done.after(l, phase, h, 2))
                ordered = in_group(1, pair[1][:])
                late, early = by_group(1, acc[:, 256:SEQ]), by_group(1, acc[:, 0:256])
                dve.tensor_tensor(late, late, ordered[:, :, 0:192], ALU.add).then_inc(asm_step.sem, 1)
                dve.tensor_tensor(early, early, ordered[:, :, 192:256], ALU.add).then_inc(pair_free[1].sem, 1)
                pv_free = 5 if last else 6
                dve.wait_ge(asm_step.sem, asm_step.after(l, phase, h, 1))
                dve.wait_ge(pair_free[1].sem, pair_free[1].after(l, phase, h, pv_free))
                dve.wait_ge(pv_done.sem, pv_done.after(l, phase, h, 3))
                token = by_group(2, acc[:])
                dve.tensor_tensor(token, token, in_group(2, pair[3][:]), ALU.add).then_inc(pair_free[3].sem, 1)
                if last:
                    combine(den_in, den_step, l, phase, h, ALU.add)
                dve.wait_ge(pair_free[3].sem, pair_free[3].after(l, phase, h, 2))
                dve.tensor_tensor(acc[:], acc[:], silu_a[:], ALU.mult).then_inc(asm_step.sem, 1)
                dve.wait_ge(asm_step.sem, asm_step.after(l, phase, h, 2))
                dve.wait_ge(rden_in.sem, rden_in.after(l, phase, h, 1))
                dve.tensor_tensor(acc[:], acc[:], rden[:], ALU.mult).then_inc(asm_step.sem, 1)
                dve.wait_ge(ya_hi.sem, ya_hi.after(l, phase, h, 1))
                slot = HEADS_PER_GROUP - 1 if last else h
                dve.scalar_tensor_tensor(out=tile_of(yal, slot), in0=acc[:], scalar=0.5,
                                         in1=tile_of(yah, slot).bitcast(F32), op0=ALU.mult, op1=ALU.subtract)\
                    .then_inc(ya_lo.sem, 1)

            def merged_lo(l, m):
                dve.wait_ge(mh_ready.sem, mh_ready.after(l, "AMIXL", 0, m + 1))
                dve.tensor_tensor(ml[:, m, :], stream[:, m, :], mh[:, m, :].bitcast(F32), ALU.subtract)\
                    .then_inc(ml_dve.sem, 1)

            def add_residual(l, phase, i, p, n):
                dve.wait_ge(job_done.sem, job_done.after(l, phase, i, p + 1))
                dve.wait_ge(xold_in[p].sem, xold_in[p].after(l, phase, i, 1))
                dve.scalar_tensor_tensor(out=tile_of(stream, n), in0=pair[p][:], scalar=0.5, in1=xold[:, p, :],
                                         op0=ALU.mult, op1=ALU.add).then_inc(pair_free[p].sem, 1)
                if phase == "WOUTL" and p == 1:
                    dve.wait_ge(sq_ready.sem, sq_ready.after(l, phase, i, 2))
                    dve.wait_ge(sumsq_step.sem, sumsq_step.after(l, phase, i, 1))
                    dve.tensor_tensor(sumsq[:], sumsq[:], sq[:, p, :], ALU.add).then_inc(sumsq_step.sem, 1)
                dve.wait_ge(xg_hi.sem, xg_hi.after(l, phase, i, p + 1))
                gain_lo(tile_of(stream, n), n, l * KT + (KT + n))

            for n in range(KT):
                dve.wait_ge(xg_hi.sem, n + 1)
                gain_lo(stream[:, n, :], n, n)
                if n in SQUARE_POOL:
                    m = SQUARE_POOL.index(n)
                    dve.wait_ge(sq_pool_ready, m + 1)
                    squares = sq_pool[:, m, :]
                else:
                    m = SQUARE_ACT.index(n)
                    dve.wait_ge(sq_ready.sem, m + 1)
                    squares = sq[:, m % 2, :]
                dve.wait_ge(sumsq_step.sem, n + 1)
                dve.tensor_tensor(sumsq[:], sumsq[:], squares, ALU.add).then_inc(sumsq_step.sem, 1)
            dve.wait_ge(const_in, 32)

            with dve.Fori(0, DEPTH) as l:
                dve.tensor_copy(par[:], tile_of(par_all, l)).then_inc(par_step.sem, 1)
                prepare(l)
                normalise(l)
                for t in range(2):
                    conv(l, "PRE", 0, 0, t)
                for t in range(2):
                    dve.wait_ge(xc_hi.sem, xc_hi.after(l, "PRE", 0, t + 1))
                    dve.tensor_tensor(yl[:, t, :], xc[:, t, :], yh[:, t, :].bitcast(F32), ALU.subtract)\
                        .then_inc(xc_lo.sem, 1)
                with dve.Fori(0, 3) as b:
                    lru(l, "LRU", b, b, False)
                lru(l, "LRUL", 0, 3, True)
                with dve.Fori(0, 2) as i:
                    for k in range(2):
                        mix_lru(l, "LMIX", i, k, i * 2 + (2 + k))
                for k, m in enumerate((0, 1, 6, 7)):
                    mix_lru(l, "LMIXL", 0, k, m)
                with dve.Fori(0, 3) as h:
                    attention(l, "ATT", h, False)
                attention(l, "ATTL", 0, True)
                with dve.Fori(0, 3) as i:
                    for p in range(2):
                        mix_att(l, "AMIX", i, p, i * 2 + p)
                for p in range(2):
                    mix_att(l, "AMIXL", 0, p, KT - 2 + p)
                for m in ML_DVE:
                    merged_lo(l, m)
                with dve.Fori(0, 3) as i:
                    for p in range(2):
                        add_residual(l, "WOUT", i, p, i * 2 + p)
                for p in range(2):
                    add_residual(l, "WOUTL", 0, p, KT - 2 + p)
            normalise(DEPTH, final=True)

        @block.tensor
        def _(pe):
            def product(out, k, high, low, ks, begin=True, end=True, ready=None):
                for n in ks:
                    if ready:
                        ready(n)
                    columns = slice(n * P, (n + 1) * P)
                    for w, x, first, final in ((wh, high, True, False), (wh, low, False, False), (wl, high, False, True)):
                        for s in range(2):
                            token = slice(s * HALF, (s + 1) * HALF)
                            e = pe.matmul(out[:, token], w[:, k % 2, columns], x[:, n, token],
                                          start=begin and first and n == ks[0],
                                          stop=end and final and n == ks[-1])
                return e

            def dense(l, phase, i, k, use, high=xh, low=xl, tiles=KT, done=None, ready=None):
                pe.wait_ge(w_lo.sem, w_lo.after(l, phase, i, k + 1))
                q = pair_free[k % 2]
                pe.wait_ge(q.sem, q.after(l, phase, i, use))
                product(pair[k % 2], k, high, low, range(tiles), ready=ready).then_inc(job_done.sem, 1)

            def sum_squares(l):
                pe.wait_ge(sumsq_step.sem, sumsq_step.after(l, "PRE", 0, 0))
                for n in range(2):
                    pe.wait_ge(bank_free[n].sem, bank_free[n].after(l, "PRE", 0, 0))
                pe.wait_ge(pair_free[2].sem, pair_free[2].after(l, "PRE", 0, 0))
                for n in range(KT):
                    e = pe.matmul(pair[2][:, n:n + 1], sumsq[:, n * P:(n + 1) * P], ones[:, 0:1], start=True, stop=True)
                e.then_inc(norm_done.sem, 1)

            def spread_inverse(l):
                pe.wait_ge(norm_step.sem, norm_step.after(l, "PRE", 0, 2))
                pe.wait_ge(pair_free[3].sem, pair_free[3].after(l, "PRE", 0, 0))
                for s in range(2):
                    e = pe.matmul(pair[3][:, s * HALF:(s + 1) * HALF], ones[:],
                                  diag[:, s * KT // 2:(s + 1) * KT // 2, :].rearrange("p a c -> p (a c)"),
                                  start=True, stop=True)
                e.then_inc(norm_done.sem, 1)

            def rg(l, phase, i, b, d):
                k = 2 + d
                pe.wait_ge(w_lo.sem, w_lo.after(l, phase, i, k + 1))
                for t in range(2):
                    for which in range(2):
                        o = d * 4 + t * 2 + which
                        q = pair_free[(2 + o) % 4]
                        pe.wait_ge(q.sem, q.after(l, phase, i, RG_FREES[o] - 1))
                        for n in range(TPB):
                            at_w = which * 2 * BLOCK_W + n * BLOCK_W + t * P
                            for w, x, first, final in ((wh, yh, True, False), (wh, yl, False, False),
                                                       (wl, yh, False, True)):
                                for s in range(2):
                                    token = slice(s * HALF, (s + 1) * HALF)
                                    if isinstance(b, int):
                                        moving = x[:, b * TPB + n, token]
                                    else:
                                        moving = x[:, bass.ds(b * TPB + n, 1), token].rearrange("p a s -> p (a s)")
                                    e = pe.matmul(pair[(2 + o) % 4][:, token], w[:, k % 2, at_w:at_w + P], moving,
                                                  start=first and n == 0, stop=final and n == TPB - 1)
                        e.then_inc(rg_done.sem, 1)

            def lru(l, phase, i, b, last, ready=None):
                for k in range(2):
                    dense(l, phase, i, k, 0, ready=ready if k == 0 else None)
                if last:
                    pe.wait_ge(xc_lo.sem, xc_lo.after(l, "LRUL", 0, 0))
                else:
                    pe.wait_ge(xc_lo.sem, xc_lo.after(l, phase, i, 0))
                rg(l, phase, i, b, 0)
                rg(l, phase, i, b, 1)
                for k in range(4, JOBS[phase]):
                    dense(l, phase, i, k, k // 2 + 1)

            def bank_use(l, phase, h, use):
                b = bank_free[use % 2]
                pe.wait_ge(b.sem, b.after(l, phase, h, use // 2))

            def score(l, phase, h, g):
                for n, u in enumerate(UNITS_OF[g]):
                    use = SCORES_AT[g] + n
                    bank_use(l, phase, h, use)
                    for _, kind, idx, column, width, stat in UNITS[u]:
                        out = bank[use % 2][:, column:column + width]
                        length = SEQ // DILATION[g]
                        if kind == "mid":
                            key = idx * P if g == 0 else idx * length
                            e = pe.matmul(out, qT[:, key + 64:key + 64 + P], kT[:, key:key + 2 * P], start=True, stop=True)
                        elif kind == "full":
                            e = pe.matmul(out, qT[:, idx * P:(idx + 1) * P], kT[:, idx * P:(idx + 1) * P],
                                          start=True, stop=True)
                        else:
                            first, end = idx * length, (idx + 1) * length
                            pe.matmul(out[0:64, :], qT[:, end - 64:end], kT[:, end - P:end], start=True, stop=True)
                            e = pe.matmul(out[64:128, :], qT[:, first:first + 64], kT[:, first:first + P],
                                          start=True, stop=True)
                    e.then_inc(unit_ready.sem, 1)

            def turn_values(l, phase, h, g):
                for n in range(2):
                    use = VT_AT[g] + n
                    bank_use(l, phase, h, use)
                    for c in range(4):
                        e = pe.transpose(bank[use % 2][:, c * P:(c + 1) * P],
                                         vT[:, (4 * n + c) * P:(4 * n + c + 1) * P], ident[:])
                    e.then_inc(unit_ready.sem, 1)

            def turn_probs(l, phase, h, u):
                use = PT_AT + u
                bank_use(l, phase, h, use)
                pe.wait_ge(exp_done.sem, exp_done.after(l, phase, h, u + 1))
                width = sum(t[4] for t in UNITS[u])
                for c in range(width // P):
                    e = pe.transpose(bank[use % 2][:, c * P:(c + 1) * P], scores[:, u, c * P:(c + 1) * P], ident[:])
                e.then_inc(unit_ready.sem, 1)

            def numerators(l, phase, h, u, last):
                use = PT_AT + u
                b = bank_free[use % 2]
                pe.wait_ge(b.sem, b.after(l, phase, h, use // 2 + 1))
                g = UNITS[u][0][0]
                out = pair[(3, 1, 3)[g]]
                if u == UNITS_OF[g][0]:
                    if g == 1:
                        pe.wait_ge(pair_free[1].sem, pair_free[1].after(l, phase, h, 4 if last else 5))
                    else:
                        pe.wait_ge(pair_free[3].sem, pair_free[3].after(l, phase, h, g // 2))
                prob = pT[:, u % 3, :]
                for _, kind, idx, column, width, stat in UNITS[u]:
                    chunks = SEQ // DILATION[g] // P
                    if kind == "mid":
                        at_out = idx * P if g == 0 else idx * 2 * P
                        chunk = idx if g == 0 else 2 * idx
                        for c in range(2):
                            e = pe.matmul(out[:, at_out:at_out + P], values[:, g, chunk + c, :],
                                          prob[:, column + c * P:column + (c + 1) * P], start=c == 0, stop=c == 1)
                    elif kind == "full":
                        e = pe.matmul(out[:, idx * P:(idx + 1) * P], values[:, g, idx, :],
                                      prob[:, column:column + P], start=True, stop=True)
                    else:
                        at_out = (idx + 1) * chunks * P - P
                        for c, chunk in ((0, (idx + 1) * chunks - 1), (1, idx * chunks)):
                            e = pe.matmul(out[:, at_out + 64 * c:at_out + 64 * c + 64], values[:, g, chunk, :],
                                          prob[:, column + 64 * c:column + 64 * c + 64], start=True, stop=True)
                if u == UNITS_OF[g][-1]:
                    e.then_inc(pv_done.sem, 1)

            def output(l, phase, h, last):
                for u in range(N_UNITS):
                    if u + 2 < N_UNITS:
                        turn_probs(l, phase, h, u + 2)
                    numerators(l, phase, h, u, last)

            def attention(l, phase, h, last):
                def have(p, n):
                    pe.wait_ge(pair_free[p].sem, pair_free[p].after(l, phase, h, n))

                dense(l, phase, h, 0, 0)
                have(0, 0)
                have(1, 0)
                score(l, phase, h, 0)
                dense(l, phase, h, 1, 0)
                have(0, 1)
                turn_values(l, phase, h, 0)
                dense(l, phase, h, 2, 1)
                dense(l, phase, h, 3, 1)
                have(0, 2)
                score(l, phase, h, 1)
                dense(l, phase, h, 4, 2)
                have(1, 2)
                turn_values(l, phase, h, 1)
                dense(l, phase, h, 5, 2)
                dense(l, phase, h, 6, 3)
                have(1, 3)
                score(l, phase, h, 2)
                dense(l, phase, h, 7, 3)
                have(0, 4)
                turn_values(l, phase, h, 2)
                dense(l, phase, h, 8, 4)
                for u in range(2):
                    turn_probs(l, phase, h, u)
                if last:
                    output(l, phase, h, last)
                    dense(l, phase, h, 9, 5)
                else:
                    dense(l, phase, h, 9, 4)
                    output(l, phase, h, last)

            def out_job(l, i):
                pe.wait_ge(w_lo.sem, w_lo.after(l, "WOUT", i, 1))
                pe.wait_ge(pair_free[0].sem, pair_free[0].after(l, "WOUT", i, 0))
                for x in (mh, ml):
                    for n in range(KT):
                        if x is ml:
                            ready, at = (ml_pool, ML_POOL) if n in ML_POOL else (ml_dve, ML_DVE)
                            pe.wait_ge(ready.sem, ready.after(l, "AMIXL", 0, at.index(n) + 1))
                        else:
                            pe.wait_ge(mh_ready.sem, mh_ready.after(l, "AMIXL", 0, n + 1))
                        for w in (wh, wl) if x is mh else (wh,):
                            for s in range(2):
                                token = slice(s * HALF, (s + 1) * HALF)
                                e = pe.matmul(pair[0][:, token], w[:, 0, n * P:(n + 1) * P], x[:, n, token],
                                              start=w is wh and x is mh and n == 0, stop=x is ml and n == KT - 1)
                e.then_inc(job_done.sem, 1)

            with pe.Fori(0, DEPTH) as l:
                def xg_ready(n):
                    pe.wait_ge(xg_lo.sem, xg_lo.after(l, "PRE", 0, n + 1 - KT))

                def xn_ready(n):
                    s = (xl_dve, xl_pool)[n % 2]
                    pe.wait_ge(s.sem, s.after(l, "PRE", 0, n // 2 + 1))

                dense(l, "PRE", 0, 0, 0, ready=xg_ready)
                sum_squares(l)
                pe.wait_ge(w_lo.sem, w_lo.after(l, "PRE", 0, 2))
                pe.wait_ge(pair_free[1].sem, pair_free[1].after(l, "PRE", 0, 0))
                for n in range(KT):
                    if n == SPREAD_AT:
                        spread_inverse(l)
                    product(pair[1], 1, xh, xl, [n], begin=n == 0, end=n == KT - 1)\
                        .then_inc((job_done if n == KT - 1 else x_used).sem, 1)
                with pe.Fori(0, 3) as b:
                    lru(l, "LRU", b, b, False, xn_ready)
                lru(l, "LRUL", 0, 3, True)
                hold(pe, y_lo.sem, y_lo.after(l, "LMIX", 0, 0))
                with pe.Fori(0, 2) as i:
                    for k in range(2):
                        dense(l, "LMIX", i, k, 0, yh, yl)
                    for k in range(2, 4):
                        dense(l, "LMIX", i, k, 1)
                for k in range(4):
                    dense(l, "LMIXL", 0, k, k // 2, yh, yl)
                for k in range(2):
                    dense(l, "QK", 0, k, 0)
                hold(pe, pair_free[2].sem, pair_free[2].after(l, "QK", 0, 0))
                with pe.Fori(0, 3) as h:
                    attention(l, "ATT", h, False)
                attention(l, "ATTL", 0, True)
                hold(pe, ya_lo.sem, ya_lo.after(l, "ATTL", 0, 0))

                def last_slot(n):
                    if n == ATT_KT - 1:
                        pe.wait_ge(ya_lo.sem, ya_lo.after(l, "AMIX", 0, 0))

                with pe.Fori(0, 3) as i:
                    for k in range(2):
                        dense(l, "AMIX", i, k, 0, yah, yal, ATT_KT, ready=last_slot)
                    for k in range(2, 4):
                        dense(l, "AMIX", i, k, 1)
                for k in range(2):
                    dense(l, "AMIXL", 0, k, 0, yah, yal, ATT_KT)

                with pe.Fori(0, 3) as i:
                    out_job(l, i)
                    dense(l, "WOUT", i, 1, 0, mh, ml)
                for k in range(2):
                    dense(l, "WOUTL", 0, k, 0, mh, ml)
            sum_squares(DEPTH)
            spread_inverse(DEPTH)


def _starts(per):
    start, total = {}, 0
    for name, times in PHASES:
        start[name] = total
        total += per[name] * times
    return start


JOBS_START = _starts(JOBS)
RG_FREES = [1, 1, 2, 2, 2, 2, 3, 3]
PAIR_LRU = [4, 4]


def _block(w):
    k, n = w.shape
    return w.reshape(k // P, P, n).transpose(1, 0, 2).reshape(P, k // P * n)


def _columns(v):
    return v.reshape(-1, KT, P).transpose(2, 0, 1).reshape(P, -1)


def _bias_tables():
    n_heads = N_GROUPS * HEADS_PER_GROUP
    slopes = np.float32(2.0) ** (np.float32(-8.0) * np.arange(1, n_heads + 1, dtype=np.float32) / np.float32(n_heads))
    row, key = np.arange(P)[:, None], np.arange(2 * P)[None, :]
    mid = key - (row + 64)
    edge = key[:, :P] - np.where(row < 64, row + 64, row - 64)
    full = np.where(row // 64 == key[:, :P] // 64, key[:, :P] - row, 10 * P)
    table = np.zeros((HEADS_PER_GROUP, P, N_BIAS), np.float32)
    for (g, kind), at in BIAS_AT.items():
        delta = np.abs({"mid": mid, "edge": edge, "full": full}[kind])
        for h in range(HEADS_PER_GROUP):
            bias = -slopes[g * HEADS_PER_GROUP + h] * (delta * DILATION[g]).astype(np.float32)
            table[h, :, at:at + delta.shape[1]] = np.where(delta <= WINDOW_HALF, bias, np.float32(MASKED))
    return table


def kernel(x, norm_g, w_in, b_gate, conv_w, conv_b, rg_w_a, rg_b_a, rg_w_x, rg_b_x, rg_lam, w_o_att, w_o_lru, w_out,
           final_g):
    import concourse.bacc as bacc
    from concourse.bass_utils import run_bass_kernel_spmd

    named = {"w_in": np.asarray(w_in), "w_o_att": np.asarray(w_o_att), "w_o_lru": np.asarray(w_o_lru),
             "w_out": np.asarray(w_out)}
    rg_a, rg_x = np.asarray(rg_w_a), np.asarray(rg_w_x)
    blocks = np.zeros((DEPTH * N_JOBS + JOBS["PRE"], P, KT * P), np.float32)
    for l in range(DEPTH):
        for j, what in enumerate(job_columns()):
            if what[0] == "rg":
                _, b, d = what
                blocks[l * N_JOBS + j, :, 0:2 * BLOCK_W] = _block(rg_a[l, d, b])
                blocks[l * N_JOBS + j, :, 2 * BLOCK_W:] = _block(rg_x[l, d, b])
            else:
                part = _block(named[what[0]][l][:, what[1]:what[1] + P])
                blocks[l * N_JOBS + j, :, 0:part.shape[1]] = part
    params = np.stack([np.concatenate([_columns(np.asarray(v)[l]) for v in
                                       (conv_w, conv_b, b_gate, rg_b_a, rg_b_x, rg_lam)], axis=1)
                       for l in range(DEPTH)], axis=1)
    arrays = {
        "xT": np.ascontiguousarray(np.asarray(x)[0].T).reshape(KT, P, SEQ),
        "blocks": blocks,
        "params": np.ascontiguousarray(params),
        "norm_table": np.ascontiguousarray(_columns(np.concatenate([np.asarray(norm_g), np.asarray(final_g)[None]]))),
        "bias_table": _bias_tables(),
        "identity": np.eye(P, dtype=np.float32),
    }
    nc = bacc.Bacc("TRN2", target_bir_lowering=False, num_devices=1, dynamic_dma_scratch_size=1024)
    args = [nc.dram_tensor(name, a.shape, mybir.dt.from_np(a.dtype), kind="ExternalInput").ap()
            for name, a in arrays.items()]
    out = nc.dram_tensor("outT", (KT, P, SEQ), F32, kind="ExternalOutput").ap()
    build(nc, *args, out)
    result = run_bass_kernel_spmd(nc, [arrays], core_ids=[0])
    return result.results[0]["outT"].reshape(D_MODEL, SEQ).T.reshape(1, SEQ, D_MODEL)
```
